# Optimizing a Trainium2 kernel written in Bass

```python
import math
import jax, jax.numpy as jnp
from jax import lax
import numpy as np

D_MODEL = 1024
BATCH = 1
SEQ = 512
DEPTH = 1

N_ATTN_HEADS = 8
ATTN_HEAD_DIM = 64
ATTN_WIDTH = N_ATTN_HEADS * ATTN_HEAD_DIM
MOBA_BLOCK = 256
MOBA_TOPK = 3
MOBA_QCHUNK = 64
ROPE_THETA = 10000.0
N_MLSTM_HEADS = 4
MLSTM_HEAD_DIM = 128
MLSTM_WIDTH = N_MLSTM_HEADS * MLSTM_HEAD_DIM
MLSTM_CHUNK = 64
MLSTM_CONV = 4
D_FF = 2816
FFN_CONV = 3
D_IN = 3 * ATTN_WIDTH + 4 * MLSTM_WIDTH + 2 * N_MLSTM_HEADS + 2 * D_MODEL
EPS = 1e-6
NEG = -1e30

kernel_name = "hybrid_moba_mlstm_convglu_block"

def rms_norm(x, g):
    xf = x.astype(jnp.float32)
    y = xf * lax.rsqrt(jnp.mean(xf * xf, axis=-1, keepdims=True) + EPS)
    return (y * g.astype(jnp.float32)).astype(x.dtype)

def causal_dwconv(x, w):
    width = w.shape[0]
    s = x.shape[1]
    xp = jnp.pad(x, ((0, 0), (width - 1, 0), (0, 0)))
    out = w[0] * xp[:, 0:s]
    for j in range(1, width):
        out = out + w[j] * xp[:, j:j + s]
    return out

def split_heads(t, n_heads, head_dim):
    b, s, _ = t.shape
    return t.reshape(b, s, n_heads, head_dim).transpose(0, 2, 1, 3)

def merge_heads(t):
    b, h, s, d = t.shape
    return t.transpose(0, 2, 1, 3).reshape(b, s, h * d)

def rope(t, positions):
    half = t.shape[-1] // 2
    inv_freq = ROPE_THETA ** (-(jnp.arange(half, dtype=jnp.float32) / half))
    ang = positions.astype(jnp.float32)[:, None, :, None] * inv_freq
    cos, sin = jnp.cos(ang), jnp.sin(ang)
    t1 = t[..., :half].astype(jnp.float32)
    t2 = t[..., half:].astype(jnp.float32)
    return jnp.concatenate([t1 * cos - t2 * sin, t2 * cos + t1 * sin], axis=-1).astype(t.dtype)

def moba_attention(q, k, v):
    b, h, s, d = q.shape
    nb = -(-s // MOBA_BLOCK)
    pad = nb * MOBA_BLOCK - s
    kp = jnp.pad(k, ((0, 0), (0, 0), (0, pad), (0, 0))).reshape(b, h, nb, MOBA_BLOCK, d)
    vp = jnp.pad(v, ((0, 0), (0, 0), (0, pad), (0, 0))).reshape(b, h, nb, MOBA_BLOCK, d)
    k_mean = jnp.mean(kp.astype(jnp.float32), axis=3).astype(k.dtype)
    topk = min(MOBA_TOPK, nb)
    scale = 1.0 / math.sqrt(d)
    n_chunks = s // MOBA_QCHUNK
    bi = jnp.arange(b)[:, None, None, None]
    hi = jnp.arange(h)[None, :, None, None]
    blk_ids = jnp.arange(nb)

    def chunk_fn(c):
        start = c * MOBA_QCHUNK
        qc = lax.dynamic_slice_in_dim(q, start, MOBA_QCHUNK, axis=2)
        j = start // MOBA_BLOCK
        gate = jnp.einsum('bhqd,bhnd->bhqn', qc, k_mean, preferred_element_type=jnp.float32)
        gate = jnp.where(blk_ids < j, gate, NEG)
        _, idx = lax.top_k(gate, topk)
        valid = idx < j
        kg = kp[bi, hi, idx]
        vg = vp[bi, hi, idx]
        s_sel = jnp.einsum('bhqd,bhqtnd->bhqtn', qc, kg, preferred_element_type=jnp.float32) * scale
        s_sel = jnp.where(valid[..., None], s_sel, NEG).reshape(b, h, MOBA_QCHUNK, topk * MOBA_BLOCK)
        k_own = lax.dynamic_index_in_dim(kp, j, axis=2, keepdims=False)
        v_own = lax.dynamic_index_in_dim(vp, j, axis=2, keepdims=False)
        s_own = jnp.einsum('bhqd,bhkd->bhqk', qc, k_own, preferred_element_type=jnp.float32) * scale
        q_pos = start + jnp.arange(MOBA_QCHUNK)
        k_pos = j * MOBA_BLOCK + jnp.arange(MOBA_BLOCK)
        s_own = jnp.where(k_pos[None, :] <= q_pos[:, None], s_own, NEG)
        p = jax.nn.softmax(jnp.concatenate([s_sel, s_own], axis=-1), axis=-1)
        p_sel = p[..., :topk * MOBA_BLOCK].reshape(b, h, MOBA_QCHUNK, topk, MOBA_BLOCK).astype(v.dtype)
        p_own = p[..., topk * MOBA_BLOCK:].astype(v.dtype)
        return (jnp.einsum('bhqtn,bhqtnd->bhqd', p_sel, vg)
                + jnp.einsum('bhqk,bhkd->bhqd', p_own, v_own))

    out = lax.map(chunk_fn, jnp.arange(n_chunks))
    return out.transpose(1, 2, 0, 3, 4).reshape(b, h, s, d)

def mlstm_chunkwise(q, k, v, i_pre, f_pre):
    dtype = v.dtype
    b, h, s, dk = q.shape
    dv = v.shape[-1]
    nc = s // MLSTM_CHUNK
    L = MLSTM_CHUNK
    qf = q.astype(jnp.float32)
    kf = k.astype(jnp.float32) / math.sqrt(dk)
    vf = v.astype(jnp.float32)
    log_f = jax.nn.log_sigmoid(f_pre.astype(jnp.float32))
    log_i = i_pre.astype(jnp.float32)

    def chunks(t):
        t = t.reshape((b, h, nc, L) + t.shape[3:])
        return jnp.moveaxis(t, 2, 0)

    b_cum = jnp.cumsum(log_f.reshape(b, h, nc, L), axis=-1)
    xs = (chunks(qf), chunks(kf), chunks(vf), chunks(log_i), jnp.moveaxis(b_cum, 2, 0))
    tril = jnp.tril(jnp.ones((L, L), dtype=bool))

    def step(carry, inp):
        C, n, m = carry
        qc, kc, vc, ac, bc = inp
        dmat = jnp.where(tril, bc[..., :, None] - bc[..., None, :] + ac[..., None, :], NEG)
        inter = bc + m[..., None]
        m_t = jnp.maximum(inter, jnp.max(dmat, axis=-1))
        w_intra = jnp.exp(dmat - m_t[..., None])
        w_inter = jnp.exp(inter - m_t)
        scores = w_intra * jnp.einsum('bhld,bhsd->bhls', qc, kc)
        num = (w_inter[..., None] * jnp.einsum('bhld,bhdv->bhlv', qc, C)
               + jnp.einsum('bhls,bhsv->bhlv', scores, vc))
        den = w_inter * jnp.einsum('bhld,bhd->bhl', qc, n) + jnp.sum(scores, axis=-1)
        h_out = num / jnp.maximum(jnp.abs(den), jnp.exp(-m_t))[..., None]
        b_last = bc[..., -1]
        dec = b_last[..., None] - bc + ac
        m_new = jnp.maximum(b_last + m, jnp.max(dec, axis=-1))
        wk = jnp.exp(dec - m_new[..., None])
        carry_scale = jnp.exp(b_last + m - m_new)
        C_new = carry_scale[..., None, None] * C + jnp.einsum('bhs,bhsd,bhsv->bhdv', wk, kc, vc)
        n_new = carry_scale[..., None] * n + jnp.einsum('bhs,bhsd->bhd', wk, kc)
        return (C_new, n_new, m_new), h_out

    init = (jnp.zeros((b, h, dk, dv), jnp.float32), jnp.zeros((b, h, dk), jnp.float32),
            jnp.zeros((b, h), jnp.float32))
    _, hs = lax.scan(step, init, xs)
    return jnp.moveaxis(hs, 0, 2).reshape(b, h, s, dv).astype(dtype)

def setup_inputs(seed: int = 0) -> dict:
    key = jax.random.key(seed)
    ks = jax.random.split(key, 16)

    def nrm(k, shape, scale):
        return jax.random.normal(k, shape, jnp.float32) * scale

    x = nrm(ks[0], (BATCH, SEQ, D_MODEL), 1.0)
    positions = jnp.broadcast_to(jnp.arange(SEQ, dtype=jnp.int32), (BATCH, SEQ))
    return {
        "x": x,
        "positions": positions,
        "norm_mix_g": 1.0 + nrm(ks[1], (DEPTH, D_MODEL), 0.02),
        "w_in": nrm(ks[2], (DEPTH, D_MODEL, D_IN), D_MODEL ** -0.5),
        "conv_mlstm": nrm(ks[3], (DEPTH, MLSTM_CONV, 2 * MLSTM_WIDTH), MLSTM_CONV ** -0.5),
        "i_bias": nrm(ks[4], (DEPTH, N_MLSTM_HEADS), 0.1),
        "f_bias": 3.0 + nrm(ks[5], (DEPTH, N_MLSTM_HEADS), 0.5),
        "mlstm_norm_g": 1.0 + nrm(ks[6], (DEPTH, MLSTM_WIDTH), 0.02),
        "w_branch_attn": nrm(ks[7], (DEPTH, ATTN_WIDTH, D_MODEL), ATTN_WIDTH ** -0.5),
        "w_branch_mlstm": nrm(ks[8], (DEPTH, MLSTM_WIDTH, D_MODEL), MLSTM_WIDTH ** -0.5),
        "w_out": nrm(ks[9], (DEPTH, D_MODEL, D_MODEL), D_MODEL ** -0.5),
        "norm_ffn_g": 1.0 + nrm(ks[10], (DEPTH, D_MODEL), 0.02),
        "w_up": nrm(ks[11], (DEPTH, D_MODEL, 2 * D_FF), D_MODEL ** -0.5),
        "conv_ffn": nrm(ks[12], (DEPTH, FFN_CONV, 2 * D_FF), FFN_CONV ** -0.5),
        "w_down": nrm(ks[13], (DEPTH, D_FF, D_MODEL), D_FF ** -0.5),
        "norm_final_g": 1.0 + nrm(ks[14], (D_MODEL,), 0.02),
    }

def reference(x, positions, norm_mix_g, w_in, conv_mlstm, i_bias, f_bias, mlstm_norm_g,
              w_branch_attn, w_branch_mlstm, w_out, norm_ffn_g, w_up, conv_ffn, w_down,
              norm_final_g):
    sizes = [ATTN_WIDTH] * 3 + [MLSTM_WIDTH] * 4 + [N_MLSTM_HEADS] * 2 + [D_MODEL] * 2
    split_points = [int(p) for p in np.cumsum(sizes)[:-1]]
    for layer in range(DEPTH):
        h = rms_norm(x, norm_mix_g[layer])
        proj = h @ w_in[layer]
        (q_a, k_a, v_a, q_m, k_m, v_m, o_m, i_m, f_m, g_a, g_m) = jnp.split(proj, split_points, axis=-1)

        qa = rope(split_heads(q_a, N_ATTN_HEADS, ATTN_HEAD_DIM), positions)
        ka = rope(split_heads(k_a, N_ATTN_HEADS, ATTN_HEAD_DIM), positions)
        va = split_heads(v_a, N_ATTN_HEADS, ATTN_HEAD_DIM)
        y_attn = merge_heads(moba_attention(qa, ka, va)) @ w_branch_attn[layer]

        qk_m = jax.nn.silu(causal_dwconv(jnp.concatenate([q_m, k_m], axis=-1), conv_mlstm[layer]))
        qm, km = jnp.split(qk_m, 2, axis=-1)
        i_pre = (i_m + i_bias[layer]).transpose(0, 2, 1)
        f_pre = (f_m + f_bias[layer]).transpose(0, 2, 1)
        hm = mlstm_chunkwise(split_heads(qm, N_MLSTM_HEADS, MLSTM_HEAD_DIM),
                             split_heads(km, N_MLSTM_HEADS, MLSTM_HEAD_DIM),
                             split_heads(v_m, N_MLSTM_HEADS, MLSTM_HEAD_DIM), i_pre, f_pre)
        hm = rms_norm(hm, mlstm_norm_g[layer].reshape(N_MLSTM_HEADS, 1, MLSTM_HEAD_DIM))
        y_mlstm = (merge_heads(hm) * jax.nn.sigmoid(o_m)) @ w_branch_mlstm[layer]

        merged = jax.nn.sigmoid(g_a) * y_attn + jax.nn.sigmoid(g_m) * y_mlstm
        x = x + merged @ w_out[layer]

        h2 = rms_norm(x, norm_ffn_g[layer])
        u = causal_dwconv(h2 @ w_up[layer], conv_ffn[layer])
        gate, up = jnp.split(u, 2, axis=-1)
        x = x + (jax.nn.silu(gate) * up) @ w_down[layer]
    return rms_norm(x, norm_final_g)


_drawn_inputs = setup_inputs


def setup_inputs(seed=0):
    import zlib

    import numpy as np

    out = dict(_drawn_inputs(seed))
    spreads = {}
    factors = {'norm_mix_g': 4.526,
     'i_bias': 8.0,
     'mlstm_norm_g': 8.0,
     'norm_ffn_g': 4.043,
     'norm_final_g': 2.876}
    for name, (base, spread) in spreads.items():
        noise = np.random.default_rng([zlib.crc32(name.encode()), seed]).standard_normal(out[name].shape)
        drawn = base * np.exp(spread * noise) if base else spread * noise
        out[name] = __import__('jax').numpy.asarray(drawn.astype(out[name].dtype))
    for name, factor in factors.items():
        out[name] = (out[name] * factor).astype(out[name].dtype)
    return out
```

```python
from contextlib import ExitStack

import numpy as np

import concourse.bass as bass
from concourse import mybir

P = 128
F32 = mybir.dt.float32
F32R = mybir.dt.float32r
BF16 = mybir.dt.bfloat16
I32 = mybir.dt.int32
ALU = mybir.AluOpType
ACT = mybir.ActivationFunctionType
AX_X = mybir.AxisListType.X

SEQ, D = 512, 1024
NT = SEQ // P
KT = D // P
AH, AD = 8, 64
MH, MD = 4, 128
BW = 512
FF = 2816
NF = FF // P
GROUP = (12, 10)
EPS = 1e-6
NEG = -1e30
COL_IF = 7 * BW
COL_GA = COL_IF + 2 * MH
COL_GM = COL_GA + D
LOAD = 2048
TWO_PI = 6.283185307179586
ROUND = 1.5 * 2.0 ** 23

U_QA, U_KA, U_VA, U_QM, U_KM, U_VM, U_OM, U_GA0, U_GM0, U_GA1, U_B0, U_GM1, U_B1, U_O0, U_O1 = range(15)
N_UP = (2 * (U_O1 + 1), 2 * (U_O1 + 1) + GROUP[0] + GROUP[0] // 2)
N_DOWN = (N_UP[0] + GROUP[0], N_UP[1] + GROUP[1])
N_LOADS = N_DOWN[1] + GROUP[1] // 2
NBLK = 40
ATT = 8
MLS = 26


def split_12bit(value, parts):
    out = []
    for _ in range(parts):
        e = int(np.floor(np.log2(abs(value)))) - 11
        q = round(value / 2.0 ** e) * 2.0 ** e
        out.append(q)
        value -= q
    return out


class BankPlan:

    def __init__(self):
        self.at, self.uses, self.fulls = {}, [0] * 8, [0] * 8

    def use(self, tag, bank, signals_full=True):
        self.fulls[bank] += signals_full
        self.at[tag] = (bank, self.uses[bank], self.fulls[bank])
        self.uses[bank] += 1


def plan_banks():
    plan = BankPlan()
    for t in range(NT):
        for j in range(2):
            plan.use(("norm1", t, j), (2 if t % 2 == 0 else 4) + j)
    for c in range(NBLK):
        plan.use(("block", c), c % 2)
        if 1 <= c <= 8:
            plan.use(("rope", c - 1), 6 + (c - 1) % 2)
        if c == 5:
            plan.use(("gates_if",), 4)
        if c == 11:
            plan.use(("cols_if",), 7)
        if 0 <= c - ATT < 16:
            for e in range(2):
                plan.use(("score", c - ATT, e), 2 + e)
        if 0 <= c - ATT - 1 < 16:
            for e in range(2):
                plan.use(("probT", c - ATT - 1, e), 4 + e)
        if 0 <= c - ATT - 2 < 16 and (c - ATT - 2) % 4 == 0:
            plan.use(("attn", (c - ATT - 2) // 4), 6, signals_full=False)
        if 0 <= c - ATT - 6 <= 12 and (c - ATT - 6) % 4 == 0:
            plan.use(("attnT", (c - ATT - 6) // 4), 7)
        if 0 <= c - MLS < 8:
            if (c - MLS) % 2 == 0:
                plan.use(("decay", (c - MLS) // 2), 6)
            for e in range(2):
                plan.use(("mscore", c - MLS, e), 2 + e)
        if 0 <= c - MLS - 1 < 8:
            plan.use(("mnum", c - MLS - 1), 4 + (c - MLS - 1) % 2)
        if 0 <= c - MLS - 3 <= 6 and (c - MLS - 3) % 2 == 0:
            plan.use(("mT", (c - MLS - 3) // 2), 7)
    ring = 0

    def ring_use(tag):
        nonlocal ring
        plan.use(tag, ring % 4)
        ring += 1

    for n in range(4):
        ring_use(("y", n, 0))
        ring_use(("y", n, 1))
    for m in range(4):
        ring_use(("gate", m))
    for n in range(4, 8):
        ring_use(("y", n, 0))
        ring_use(("y", n, 1))
    for t in range(NT):
        for n in range(2):
            ring_use(("out", t, n))
    for t in range(NT):
        for j in range(2):
            plan.use(("norm2", t, j), (4 if t % 2 == 0 else 6) + j)
    for g in range(2):
        first = g * GROUP[0]
        for f in range(first, first + GROUP[g]):
            ring_use(("up", f, 0))
            ring_use(("up", f, 1))
        for t in range(NT):
            for n in range(2):
                plan.use(("down", g, t, n), 2 * t + n)
    return plan


def build(nc, x, positions, norm_mix_g, w_in, conv_mlstm, i_bias, f_bias, mlstm_norm_g, w_branch_attn,
          w_branch_mlstm, w_out, norm_ffn_g, w_up, conv_ffn, w_down, norm_final_g, inv_freq, out):
    plan = plan_banks().at
    x_v = x.rearrange("b (t p) d -> p (b t) d", p=P)
    out_v = out.rearrange("b (t p) d -> p (b t) d", p=P)
    w_in2 = w_in[0].rearrange("(k p) c -> p k c", p=P)
    w_out2 = w_out[0].rearrange("(k p) c -> p k c", p=P)
    w_ba = w_branch_attn[0].rearrange("(k p) c -> p k c", p=P)
    w_bm = w_branch_mlstm[0].rearrange("(k p) c -> p k c", p=P)
    w_up2 = w_up[0].rearrange("(k p) c -> p k c", p=P)
    w_dn = w_down[0].rearrange("(k p) c -> p k c", p=P)

    ctx = ExitStack()
    with ctx:
        base = [-(-nc.sbuf_base // 64) * 64]
        ctx.enter_context(nc.sbuf_tensor("arena", [P, (nc.sbuf_usable_end - base[0] - 64) // 4], F32))

        def region(nbytes):
            at = base[0]
            base[0] += -(-nbytes // 32) * 32
            assert base[0] <= nc.sbuf_usable_end - 32, base
            return at

        def place(name, shape, dt, at):
            return nc.alloc_sbuf_tensor_at(name, shape, dt, offset=at)

        raw = place("w_raw", [P, 2, LOAD], F32, region(16384))
        w_hi = place("w_hi", [P, 4, LOAD], F32R, region(32768))
        w_lo = place("w_lo", [P, 4, LOAD], F32R, region(32768))
        at_h = region(32768)
        hT_hi = place("hT_hi", [P, KT, SEQ], F32R, at_h)
        hT_lo = place("hT_lo", [P, KT, SEQ], F32R, at_h + 16384)
        out_sb = place("out_sb", [P, NT, D], F32, at_h)
        gF = place("gF", [P, D], F32, at_h + 16384)
        at_x = region(16384)
        x_sb = place("x_sb", [P, NT, D], F32, at_x)
        rows = place("rows", [4, 8, SEQ], F32, at_x)
        o_sig = place("o_sig", [P, NT, BW], F32, at_x)
        tok_a = place("tok_a", [P, 2, BW], F32, at_x + 8192)
        gate_m = place("gate_m", [P, 4, SEQ], F32, at_x + 8192)
        mrg_lo1 = place("mrg_lo1", [P, 4, SEQ], F32R, at_x)
        cv = place("cv", [P, 2, 2, SEQ], F32, at_x)
        sil = place("sil", [P, 2, SEQ], F32, at_x + 8192)
        at_a = region(16384)
        qT = place("qT", [P, 4, SEQ], F32, at_a)
        kT = place("kT", [P, 4, SEQ], F32, at_a + 8192)
        hmT_hi = place("hmT_hi", [P, 4, SEQ], F32R, at_a)
        hmT_lo = place("hmT_lo", [P, 4, SEQ], F32R, at_a + 8192)
        x2 = place("x2", [P, NT, D], F32, at_a)
        at_b = region(16384)
        sq = place("sq", [P, D], F32, at_b)
        diag = place("diag", [P, NT, P], F32, at_b + 4096)
        h32 = place("h32", [P, 2, 2, 4, P], F32, at_b + 8192)
        atT_hi = place("atT_hi", [P, 4, SEQ], F32R, at_b)
        atT_lo = place("atT_lo", [P, 4, SEQ], F32R, at_b + 8192)
        at_c = region(16384)
        rp = place("rp", [P, 2, 2, BW], F32, at_c)
        qr = place("qr", [P, 2, BW], F32, at_c + 8192)
        cosT = place("cosT", [P, NT, 32], F32, at_c + 12288)
        sinT = place("sinT", [P, NT, 2, 32], F32, at_c + 12800)
        qmT = place("qmT", [P, 4, SEQ], F32, at_c)
        kmT = place("kmT", [P, 4, SEQ], F32, at_c + 8192)
        mrg_hi0 = place("mrg_hi0", [P, 4, SEQ], F32R, at_c)
        mrg_lo0 = place("mrg_lo0", [P, 4, SEQ], F32R, at_c + 8192)
        at_d = region(8192)
        trig = place("trig", [P, 8, P], F32, at_d)
        va = place("va", [P, NT, BW], F32, at_d)
        gate_a0 = place("gate_a0", [P, 4, SEQ], F32, at_d)
        mrg_hi1 = place("mrg_hi1", [P, 4, SEQ], F32R, at_d)
        at_e = region(NT * MH * (MD + 1) * 4)
        wif_hi = place("wif_hi", [P, KT, P], F32R, at_e)
        wif_lo = place("wif_lo", [P, KT, P], F32R, at_e + 4096)
        cacc = place("cacc", [P, 2, SEQ], F32, at_e)
        cth = place("cth", [P, 2, SEQ], F32, at_e + 4096)
        vm = place("vm", [P, NT, MH, MD + 1], F32, at_e)
        gate_a1 = place("gate_a1", [P, 4, SEQ], F32, at_e)
        act_hi = place("act_hi", [P, GROUP[0], SEQ], F32R, at_b)
        act_lo = place("act_lo", [P, GROUP[0], SEQ], F32R, at_b + GROUP[0] * SEQ * 4)
        assert at_b + 2 * GROUP[0] * SEQ * 4 <= at_e + 8256

        def small(name, shape, dt):
            n = 4 if dt != BF16 else 2
            for s in shape[1:]:
                n *= s
            return place(name, shape, dt, region(n))

        prob = small("prob", [P, 2, SEQ], F32)
        probT = small("probT", [P, 2, SEQ], F32)
        em = probT
        ident = small("ident", [P, P], F32)
        ident_b = small("ident_b", [P, P], BF16)
        mask_ts = small("mask_ts", [P, P], BF16)
        mask_st = small("mask_st", [P, P], F32)
        ones_r = small("ones_r", [4, P], F32)
        neg_m = small("neg_m", [4, SEQ], F32)
        gcol = small("gcol", [P, 56], F32)
        expm = small("expm", [P, 16], F32)
        par_a = small("par_a", [P, 96], F32)
        par_b = small("par_b", [P, 88], F32)
        wif_raw = small("wif_raw", [P, KT, 8], F32)
        stg_a = place("stg_a", [96, P], F32, at_d + 4096)
        stg_b = place("stg_b", [88, P], F32, at_d + 4608)
        pos_i = small("pos_i", [P, NT], I32)
        pos_f = small("pos_f", [P, NT], F32)
        invf = small("invf", [P, 32], F32)
        bias_if = small("bias_if", [36, 1], F32)
        ss = small("ss", [P, 16], F32)
        var = small("var", [P, 4], F32)
        seed_i = small("seed_i", [P, 4], I32)
        rstd = small("rstd", [P, 4], F32)
        newt = small("newt", [P, 4], F32)
        nmax = small("nmax", [P, 2, 2], F32)
        rsum = small("rsum", [P, 2, AH], F32)
        rinv = small("rinv", [P, AH], F32)
        den = small("den", [P, 2], F32)
        dinv = small("dinv", [P, 2], F32)
        carry = small("carry", [4, NT], F32)
        junk = small("junk", [P, 2, P], F32)
        g1T, g2T = par_a[:, 0:8], par_a[:, 8:16]
        mgT = par_a[:, 48:52]

        def tap_m(j, c):
            return par_a[:, 16 + 8 * j + c:17 + 8 * j + c]

        def tap_f(j, c):
            if j == 2:
                return par_a[:, bass.ds(52 + c, 1)]
            return par_b[:, bass.ds(2 * NF * j + c, 1)]

        ps = ctx.enter_context(nc.psum_tensor("ps", [P, 8, 512], F32))

        def sem(name):
            return ctx.enter_context(nc.semaphore(name))

        bank_full = [sem(f"bank_full{b}") for b in range(8)]
        bank_free = [sem(f"bank_free{b}") for b in range(8)]
        raw_loaded = [sem(f"raw_loaded{i}") for i in range(2)]
        hi_ready, lo_ready = sem("hi_ready"), sem("lo_ready")
        x_loaded = [sem(f"x_loaded{t}") for t in range(NT)]
        x_again = sem("x_again")
        params_loaded, rest_loaded = sem("params_loaded"), sem("rest_loaded")
        pos_loaded, wif_loaded = sem("pos_loaded"), sem("wif_loaded")
        gf_loaded, out_stored = sem("gf_loaded"), sem("out_stored")
        consts = sem("consts")
        wif_zeroed, wif_hi_ready, wif_ready = sem("wif_zeroed"), sem("wif_hi_ready"), sem("wif_ready")
        stage_T, params_ready = sem("stage_T"), sem("params_ready")
        sumsq_ready, diag_ready, h_hi_ready, hT_ready = sem("sumsq_ready"), sem("diag_ready"), sem("h_hi_ready"), sem("hT_ready")
        angles_ready, trig_ready = sem("angles_ready"), sem("trig_ready")
        rope_done = sem("rope_done")
        f_row, f_abs, f_ln, rows_ready, expm_ready = sem("f_row"), sem("f_abs"), sem("f_ln"), sem("rows_ready"), sem("expm_ready")
        max_ready, pv_done, tok_ready, at_hi_ready, atT_ready = (
            sem("max_ready"), sem("pv_done"), sem("tok_ready"), sem("at_hi_ready"), sem("atT_ready"))
        conv_tap, conv_tanh, conv_done = sem("conv_tap"), sem("conv_tanh"), sem("conv_done")
        ones_col = sem("ones_col")
        o_tanh, o_ready = sem("o_tanh"), sem("o_ready")
        em_ready, decay_ready, hm_raw, hm_sq, hm_ready = (
            sem("em_ready"), sem("decay_ready"), sem("hm_raw"), sem("hm_sq"), sem("hm_ready"))
        hm_hi_ready, hmT_ready = sem("hm_hi_ready"), sem("hmT_ready")
        m32_ready, mrg_hi_ready, mrg_ready = sem("m32_ready"), sem("mrg_hi_ready"), sem("mrg_ready")
        glu_tap, glu_silu, glu_prod, glu_hi, act_ready = (
            sem("glu_tap"), sem("glu_silu"), sem("glu_prod"), sem("glu_hi"), sem("act_ready"))
        down_used = sem("down_used")
        final_sq, out_ready = sem("final_sq"), sem("out_ready")
        dve_step, act_step, pool_step = sem("dve_step"), sem("act_step"), sem("pool_step")

        def wait_full(eng, tag):
            bank, _, full = plan[tag]
            eng.wait_ge(bank_full[bank], full)

        def wait_freed(eng, tag):
            bank, k, _ = plan[tag]
            eng.wait_ge(bank_free[bank], k + 1)

        def wait_bank(eng, tag):
            bank, k, _ = plan[tag]
            if k:
                eng.wait_ge(bank_free[bank], k)

        def B(tag):
            return ps[:, plan[tag][0], :]

        def fullsem(tag):
            return bank_full[plan[tag][0]]

        def freesem(tag):
            return bank_free[plan[tag][0]]

        class Steps:

            def __init__(self, eng, s):
                self.eng, self.s, self.n = eng, s, 0

            def mark(self, ins):
                ins.then_inc(self.s, 1)
                self.n = self.n + 1
                return self.n

            def link(self, ins):
                self.eng.wait_ge(self.s, self.mark(ins))

        UNIT_LAST = {}
        for u in range(U_GA1 + 1):
            UNIT_LAST[u] = ("block", 4 * u + 3)
        UNIT_LAST[U_B0], UNIT_LAST[U_GM1], UNIT_LAST[U_B1] = ("y", 3, 1), ("gate", 3), ("y", 7, 1)
        UNIT_LAST[U_O0], UNIT_LAST[U_O1] = ("out", 3, 0), ("out", 3, 1)

        def wait_slot(eng, n):
            m = n - 4
            if m < 0:
                return
            if m in (2 * U_B0, 2 * U_B1):
                wait_full(eng, ("y", 3 if m == 2 * U_B0 else 7, 0))
                return
            if m < N_UP[0]:
                wait_full(eng, UNIT_LAST[m // 2])
                return
            for g in range(2):
                if N_UP[g] <= m < N_DOWN[g]:
                    wait_full(eng, ("up", g * GROUP[0] + m - N_UP[g], 1))
                    return
                last = N_DOWN[g] + GROUP[g] // 2 - 1
                if N_DOWN[g] <= m < last:
                    eng.wait_ge(down_used, (GROUP[0] // 2 - 1) * g + m - N_DOWN[g] + 1)
                    return
                if m == last:
                    wait_full(eng, ("down", g, 3, 1))
                    return

        block = ctx.enter_context(nc.Block())

        @block.sync
        def _(sp):
            def load(n, parts, wait=True):
                if n >= 2 and wait:
                    sp.wait_ge(lo_ready, n - 1)
                for k, (src, shape) in enumerate(parts):
                    dst = raw[:, n % 2, k * 1024:(k + 1) * 1024].rearrange("p (k c) -> p k c", k=shape)
                    sp.dma_start(dst, src).then_inc(raw_loaded[n % 2], 16)

            def rect(w, k0, c0, cols):
                k = 1024 // cols
                return [(w[:, k0 + i * k:k0 + (i + 1) * k, c0:c0 + cols], k) for i in range(2)]

            def unit(u, w, c0):
                for half in range(2):
                    load(2 * u + half, rect(w, 4 * half, c0, BW))

            sp.dma_start(x_sb[:, 0, :], x_v[:, 0, :]).then_inc(x_loaded[0], 16)
            load(0, rect(w_in2, 0, 0, BW))
            for t in range(1, NT):
                sp.dma_start(x_sb[:, t, :], x_v[:, t, :]).then_inc(x_loaded[t], 16)
                if t == 1:
                    load(1, rect(w_in2, 4, 0, BW))
            for u in range(U_KA, U_OM + 1):
                unit(u, w_in2, u * BW)
            unit(U_GA0, w_in2, COL_GA)
            unit(U_GM0, w_in2, COL_GM)
            unit(U_GA1, w_in2, COL_GA + BW)
            load(2 * U_B0, rect(w_ba, 0, 0, BW))
            load(2 * U_B0 + 1, rect(w_bm, 0, 0, BW))
            unit(U_GM1, w_in2, COL_GM + BW)
            load(2 * U_B1, rect(w_ba, 0, BW, BW))
            load(2 * U_B1 + 1, rect(w_bm, 0, BW, BW))
            unit(U_O0, w_out2, 0)
            unit(U_O1, w_out2, BW)
            for g in range(2):
                with sp.Fori(0, GROUP[g] // 2) as it:
                    for j in range(2):
                        n = N_UP[g] + j
                        sp.wait_ge(lo_ready, 2 * it + (n - 1))
                        col = (2 * it + (g * GROUP[0] + j)) * P
                        for s in range(2):
                            dst = raw[:, n % 2, s * 1024:(s + 1) * 1024].rearrange("p (k c) -> p k c", k=KT)
                            sp.dma_start(dst, w_up2[:, :, bass.ds(col + s * FF, P)]).then_inc(raw_loaded[n % 2], 16)
                for d in range(GROUP[g] // 2):
                    k0 = g * GROUP[0] + 2 * d
                    load(N_DOWN[g] + d, [(w_dn[:, k0 + i:k0 + i + 1, :], 1) for i in range(2)])
            for t in range(NT):
                sp.wait_ge(out_ready, t + 1)
                sp.dma_start(out_v[:, t, :], out_sb[:, t, :]).then_inc(out_stored, 16)
            sp.wait_ge(out_stored, 16 * NT)

        @block.gpsimd
        def _(pool):
            steps = Steps(pool, pool_step)
            steps.link(pool.memset(ident[:, :], 0.0))
            pool.affine_select(out=ident[:, :], in_=ident[:, :], compare_op=ALU.not_equal, fill=1.0, base=0,
                               pattern=[[-1, P]], channel_multiplier=1).then_inc(consts, 1)
            pool.dma_start(stg_a[16:48, :], conv_mlstm[0].rearrange("j (c p) -> (j c) p", p=P)).then_inc(rest_loaded, 16)
            pool.dma_start(stg_a[48:52, :], mlstm_norm_g[0].rearrange("(k p) -> k p", p=P)).then_inc(rest_loaded, 16)
            pool.dma_start(stg_a[52:96, :], conv_ffn[0, 2].rearrange("(c p) -> c p", p=P)).then_inc(rest_loaded, 16)
            pool.dma_start(stg_b[:, :], conv_ffn[0, 0:2].rearrange("j (c p) -> (j c) p", p=P)).then_inc(rest_loaded, 16)
            pool.dma_start(pos_i[:, :], positions.rearrange("o (t p) -> p (o t)", p=P),
                           allow_slow_non_contiguous=True).then_inc(pos_loaded, 16)
            pool.dma_start(invf[:, :], inv_freq[0].partition_broadcast(P)).then_inc(pos_loaded, 16)
            pool.dma_start(bias_if[0:4, :], i_bias.rearrange("o h -> h o")).then_inc(pos_loaded, 16)
            pool.dma_start(bias_if[32:36, :], f_bias.rearrange("o h -> h o")).then_inc(pos_loaded, 16)
            pool.dma_start(wif_raw[:, :, :], w_in2[:, :, COL_IF:COL_IF + 8]).then_inc(wif_loaded, 16)
            pool.memset(wif_hi[:, :, :].bitcast(F32), 0.0)
            pool.memset(wif_lo[:, :, :].bitcast(F32), 0.0).then_inc(wif_zeroed, 1)
            pool.memset(mask_ts[:, :], 0.0)
            pool.memset(mask_st[:, :], 0.0)
            pool.wait_ge(consts, 1)
            steps.link(pool.tensor_copy(ident_b[:, :], ident[:, :]))
            steps.link(pool.affine_select(out=mask_ts[:, :], in_=mask_ts[:, :], compare_op=ALU.is_ge, fill=NEG,
                                          base=0, pattern=[[-1, P]], channel_multiplier=1))
            steps.link(pool.affine_select(out=mask_st[:, :], in_=mask_st[:, :], compare_op=ALU.is_ge, fill=NEG,
                                          base=0, pattern=[[1, P]], channel_multiplier=-1))
            pool.memset(ones_r[:, :], 1.0).then_inc(consts, 1)
            ang, a_hi, a_lo, acc, t0, t1 = (trig[:, s, :] for s in (2, 3, 4, 0, 5, 6))
            pool.wait_ge(pos_loaded, 64)
            steps.link(pool.tensor_copy(pos_f[:, :], pos_i[:, :]))
            steps.link(pool.tensor_tensor(ang.rearrange("p (t c) -> p t c", t=NT),
                                   pos_f[:, :].unsqueeze(2).to_broadcast([P, NT, 32]),
                                   invf[:, :].unsqueeze(1).to_broadcast([P, NT, 32]), ALU.mult))
            steps.link(pool.tensor_scalar(t0, ang, 4097.0, None, ALU.mult))
            steps.link(pool.tensor_tensor(t1, t0, ang, ALU.subtract))
            steps.link(pool.tensor_tensor(a_hi, t0, t1, ALU.subtract))
            steps.link(pool.tensor_tensor(a_lo, ang, a_hi, ALU.subtract))
            c1, c2, c3, c4 = split_12bit(1.0 / TWO_PI, 4)
            steps.link(pool.tensor_scalar(acc, a_hi, c4, None, ALU.mult))
            for part, c in ((a_lo, c3), (a_hi, c3), (a_lo, c2)):
                steps.link(pool.tensor_scalar(t0, part, c, None, ALU.mult))
                steps.link(pool.tensor_tensor(acc, acc, t0, ALU.add))
            for part, c in ((a_lo, c1), (a_hi, c2), (a_hi, c1)):
                steps.link(pool.tensor_scalar(t0, part, c, None, ALU.mult))
                steps.link(pool.tensor_scalar(t1, t0, ROUND, -ROUND, ALU.add, ALU.add))
                steps.link(pool.tensor_tensor(t0, t0, t1, ALU.subtract))
                steps.link(pool.tensor_tensor(acc, acc, t0, ALU.add))
            for dst, shift in ((trig[:, 1, :], 0.25), (acc, 0.0)):
                steps.link(pool.tensor_scalar(t0, acc, shift, None, ALU.add))
                steps.link(pool.tensor_scalar(t1, t0, ROUND, -ROUND, ALU.add, ALU.add))
                steps.link(pool.tensor_tensor(t0, t0, t1, ALU.subtract))
                ins = pool.tensor_scalar(dst, t0, -0.4999999, 0.4999999, ALU.max, ALU.min)
                if shift:
                    steps.link(ins)
                else:
                    ins.then_inc(angles_ready, 1)
            pool.wait_ge(conv_done, 8)
            pool.memset(vm[:, :, :, MD:MD + 1], 1.0).then_inc(ones_col, 1)
            wait_full(pool, ("y", 7, 1))
            pool.dma_start(x2[:, :, :], x_v).then_inc(x_again, 16)
            wait_full(pool, ("up", NF - 1, 1))
            pool.dma_start(gF[:, :], norm_final_g.partition_broadcast(P)).then_inc(gf_loaded, 16)

        @block.scalar
        def _(act):
            steps = Steps(act, act_step)
            act.dma_start(stg_a[0:8, :], norm_mix_g[0].rearrange("(k p) -> k p", p=P)).then_inc(params_loaded, 16)
            act.dma_start(stg_a[8:16, :], norm_ffn_g[0].rearrange("(k p) -> k p", p=P)).then_inc(params_loaded, 16)

            def split_hi(n):
                act.wait_ge(raw_loaded[n % 2], 32 * (n // 2 + 1))
                wait_slot(act, n)
                act.activation(w_hi[:, n % 4, :], raw[:, n % 2, :], ACT.Copy).then_inc(hi_ready, 1)

            def norm_square(stage, t):
                if stage == 1:
                    act.wait_ge(x_loaded[t], 16)
                    src = x_sb
                else:
                    wait_freed(act, ("out", t, 0))
                    wait_freed(act, ("out", t, 1))
                    src = x2
                if t or stage == 2:
                    act.wait_ge(sumsq_ready, 4 * (stage - 1) + t)
                act.activation(sq[:, :], src[:, t, :], ACT.Square,
                               accum_out=ss[:, t:t + 1]).then_inc(sumsq_ready, 1)

            def norm_hi(stage, t):
                for j in range(2):
                    wait_freed(act, (f"norm{stage}", t, j))
                    act.activation(hT_hi[:, 4 * j:4 * j + 4, t * P:(t + 1) * P], h32[:, t % 2, j, :, :],
                                   ACT.Copy).then_inc(h_hi_ready, 1)

            norm_square(1, 0)
            split_hi(0)
            norm_square(1, 1)
            norm_hi(1, 0)
            norm_square(1, 2)
            norm_square(1, 3)
            split_hi(1)
            norm_hi(1, 1)
            norm_hi(1, 2)
            norm_hi(1, 3)
            act.wait_ge(wif_loaded, 16)
            act.wait_ge(wif_zeroed, 1)
            act.activation(wif_hi[:, :, 0:4], wif_raw[:, :, 0:4], ACT.Copy)
            act.activation(wif_hi[:, :, 32:36], wif_raw[:, :, 4:8], ACT.Copy).then_inc(wif_hi_ready, 1)
            act.wait_ge(angles_ready, 1)
            act.activation(cosT[:, :, :], trig[:, 1, :].rearrange("p (t c) -> p t c", t=NT), ACT.Sin, scale=TWO_PI)
            act.activation(sinT[:, :, 0, :], trig[:, 0, :].rearrange("p (t c) -> p t c", t=NT), ACT.Sin, scale=-TWO_PI)
            act.activation(sinT[:, :, 1, :], trig[:, 0, :].rearrange("p (t c) -> p t c", t=NT), ACT.Sin,
                           scale=TWO_PI).then_inc(trig_ready, 1)
            split_hi(2)
            split_hi(3)

            def attn_exp(g):
                i, hp = g // 4, g % 4
                n = (i + 1) * P
                act.wait_ge(max_ready, g + 1)
                for e in range(2):
                    if g >= 1:
                        wait_full(act, ("probT", g - 1, e))
                    if hp == 0 and e == 0 and i >= 2:
                        wait_freed(act, ("attn", i - 2))
                    h = 2 * hp + e
                    act.activation(prob[:, e, 0:n], B(("score", g, e))[:, 0:n], ACT.Exp, bias=nmax[:, g % 2, e:e + 1],
                                   accum_out=rsum[:, i % 2, h:h + 1]).then_inc(freesem(("score", g, e)), 1)

            def attn_probT(g):
                n = (g // 4 + 1) * P
                wait_full(act, ("probT", g, 0))
                if g >= 1:
                    act.wait_ge(pv_done, g)
                act.copy(probT[:, 0, 0:n], B(("probT", g, 0))[:, 0:n]).then_inc(freesem(("probT", g, 0)), 1)

            def mlstm_exp(g):
                i, hp = g // 2, g % 2
                if i == 0:
                    wait_freed(act, ("decay", 0))
                else:
                    act.wait_ge(em_ready, i)
                if g >= 1:
                    wait_full(act, ("mnum", g - 1))
                else:
                    wait_full(act, ("probT", 15, 1))
                for e in range(2):
                    h = 2 * hp + e
                    for j in range(i + 1):
                        col = 4 * (i * (i + 1) // 2 + j) + h
                        src = em[:, 0, h * P:(h + 1) * P] if j == i else B(("decay", i))[:, h * P:(h + 1) * P]
                        ins = act.activation(prob[:, e, j * P:(j + 1) * P], src, ACT.Exp, bias=gcol[:, col:col + 1])
                        if hp == 1 and e == 1 and i >= 1 and j == i - 1:
                            ins.then_inc(freesem(("decay", i)), 1)
                    ins.then_inc(decay_ready, 1)

            for c in range(NBLK):
                tag = ("block", c)
                if 12 <= c < 20:
                    m = c - 12
                    wait_full(act, tag)
                    if m >= 2:
                        act.wait_ge(conv_done, m - 1)
                    act.activation(cacc[:, m % 2, :], B(tag), ACT.Copy, scale=tap_m(3, m)).then_inc(conv_tap, 1)
                elif 8 <= c < 12:
                    wait_full(act, tag)
                    act.copy(va[:, c - 8, :], B(tag)).then_inc(freesem(tag), 1)
                elif 20 <= c < 24:
                    wait_full(act, tag)
                    if c == 20:
                        act.wait_ge(conv_done, 8)
                    act.activation(vm[:, c - 20, :, 0:MD], B(tag).rearrange("p (h d) -> p h d", h=MH),
                                   ACT.Copy).then_inc(freesem(tag), 1)
                elif 24 <= c < 28:
                    wait_full(act, tag)
                    act.activation(o_sig[:, c - 24, :], B(tag), ACT.Tanh, scale=0.5).then_inc(freesem(tag), 1)
                    wait_freed(act, tag)
                    act.activation(o_sig[:, c - 24, :], o_sig[:, c - 24, :], ACT.Copy, scale=0.5,
                                   bias=0.5).then_inc(o_ready, 1)
                elif c >= 28:
                    wait_full(act, tag)
                    dst = (gate_a0, gate_m, gate_a1)[(c - 28) // 4]
                    act.activation(dst[:, c % 4, :], B(tag), ACT.Tanh, scale=0.5).then_inc(freesem(tag), 1)
                if 1 <= c <= 8:
                    r = c - 1
                    rt = ("rope", r)
                    wait_full(act, rt)
                    dst = (qT if r < NT else kT)[:, :, (r % NT) * P:(r % NT + 1) * P]
                    act.activation(dst, B(rt).rearrange("p (h t) -> p h t", h=4), ACT.Copy,
                                   scale=0.125 if r < NT else 1.0).then_inc(freesem(rt), 1)
                if c == 8:
                    wait_full(act, ("gates_if",))
                    act.activation(rows[:, 0, :], ps[32:36, 4, :], ACT.Identity, bias=bias_if[32:36, :]).then_inc(f_row, 1)
                    act.activation(rows[:, 3, :], ps[0:4, 4, :], ACT.Identity, bias=bias_if[0:4, :]).then_inc(bank_free[4], 1)
                    act.wait_ge(f_abs, 1)
                    steps.link(act.activation(rows[:, 1, :], rows[:, 1, :], ACT.Exp, scale=-1.0))
                    act.activation(rows[:, 1, :], rows[:, 1, :], ACT.Ln, bias=1.0).then_inc(f_ln, 1)
                if c == 12:
                    wait_freed(act, ("cols_if",))
                    act.activation(expm[:, :], gcol[:, 40:56], ACT.Exp).then_inc(expm_ready, 1)
                if 0 <= c - ATT < 16:
                    attn_exp(c - ATT)
                if 0 <= c - ATT - 1 < 16:
                    attn_probT(c - ATT - 1)
                if 0 <= c - ATT - 6 <= 12 and (c - ATT - 6) % 4 == 0:
                    i = (c - ATT - 6) // 4
                    wait_full(act, ("attnT", i))
                    act.activation(atT_hi[:, :, i * P:(i + 1) * P],
                                   B(("attnT", i)).rearrange("p (k t) -> p k t", k=4), ACT.Copy).then_inc(at_hi_ready, 1)
                if 12 <= c < 20:
                    m = c - 12
                    wait_freed(act, tag)
                    act.activation(cth[:, m % 2, :], cacc[:, m % 2, :], ACT.Tanh, scale=0.5).then_inc(conv_tanh, 1)
                if 0 <= c - MLS < 8:
                    mlstm_exp(c - MLS)
                if 0 <= c - MLS - 3 <= 6 and (c - MLS - 3) % 2 == 0:
                    i = (c - MLS - 3) // 2
                    wait_freed(act, ("mT", i))
                    act.activation(hmT_hi[:, :, i * P:(i + 1) * P], em[:, 1, :].rearrange("p (k t) -> p k t", k=4),
                                   ACT.Copy).then_inc(hm_hi_ready, 1)
                if 0 <= c - MLS - 1 < 8:
                    g = c - MLS - 1
                    act.wait_ge(hm_raw, g + 1)
                    if g >= 1:
                        act.wait_ge(hm_sq, g)
                    for e in range(2):
                        h = 2 * (g % 2) + e
                        ins = act.activation(junk[:, e, :], em[:, 1, h * P:(h + 1) * P], ACT.Square,
                                             accum_out=ss[:, 4 + h:5 + h])
                    ins.then_inc(hm_sq, 1)
                if c % 4 == 3:
                    split_hi(2 * (c // 4) + 4)
                    split_hi(2 * (c // 4) + 5)

            def merge_hi(n):
                act.wait_ge(m32_ready, n + 1)
                dst = (mrg_hi0, mrg_hi1)[n // 4]
                act.activation(dst[:, n % 4, :], prob[:, n % 2, :], ACT.Copy, scale=0.5).then_inc(mrg_hi_ready, 1)

            for n in range(4):
                merge_hi(n)
            split_hi(2 * U_B0 + 4)
            split_hi(2 * U_B0 + 5)
            for m in range(4):
                wait_full(act, ("gate", m))
                if m == 0:
                    act.wait_ge(m32_ready, 4)
                act.activation(gate_m[:, m, :], B(("gate", m)), ACT.Tanh, scale=0.5).then_inc(freesem(("gate", m)), 1)
            split_hi(2 * U_GM1 + 4)
            split_hi(2 * U_GM1 + 5)
            for n in range(4, 7):
                merge_hi(n)
            split_hi(2 * U_B1 + 4)
            merge_hi(7)
            split_hi(2 * U_B1 + 5)
            for t in range(NT - 1):
                norm_square(2, t)
                norm_hi(2, t)
            split_hi(2 * U_O0 + 4)
            norm_square(2, 3)
            split_hi(2 * U_O0 + 5)
            norm_hi(2, 3)
            split_hi(2 * U_O1 + 4)
            split_hi(2 * U_O1 + 5)

            def glu(g, f, n, bank_at, it):
                f0 = g * GROUP[0]
                for s in range(2):
                    bank, _, full = plan[("up", f, s)]
                    act.wait_ge(bank_full[bank], 2 * it + full)
                    if s == 1:
                        pass
                    act.activation(cv[:, f % 2, s, :], ps[:, bank, :], ACT.Copy,
                                   scale=tap_f(2, 4 * it + (f + NF * s))).then_inc(glu_tap, 1)
                m = n + 4
                act.wait_ge(raw_loaded[m % 2], 32 * (m // 2 + 1) + 64 * it)
                act.activation(w_hi[:, m % 4, :], raw[:, m % 2, :], ACT.Copy).then_inc(hi_ready, 1)
                bank, k, _ = plan[("up", f, 0)]
                act.wait_ge(bank_free[bank], 2 * it + (k + 1))
                if f >= f0 + 2 or f >= 2:
                    act.wait_ge(act_ready, 4 * it + (f - 1))
                act.activation(sil[:, f % 2, :], cv[:, f % 2, 0, :], ACT.Silu).then_inc(glu_silu, 1)
                act.wait_ge(glu_prod, 4 * it + (f + 1))
                act.activation(act_hi[:, bass.ds(4 * it + (f - f0), 1), :], sil[:, f % 2:f % 2 + 1, :],
                               ACT.Copy).then_inc(glu_hi, 1)

            for g in range(2):
                f0, n0 = g * GROUP[0], N_UP[g]
                first = 0
                if g == 0:
                    for j in range(4):
                        glu(g, f0 + j, n0 + j, None, 0)
                    first = 4
                loops = (GROUP[g] - first) // 4
                with act.Fori(0, loops) as it:
                    for j in range(4):
                        glu(g, f0 + first + j, n0 + first + j, None, it)
                for j in range(first + 4 * loops, GROUP[g]):
                    glu(g, f0 + j, n0 + j, None, 0)
                for d in range(GROUP[g] // 2):
                    if N_DOWN[g] + d + 4 < N_LOADS:
                        split_hi(N_DOWN[g] + d + 4)
            for t in range(NT):
                for n in range(2):
                    wait_freed(act, ("down", 1, t, n))
                act.activation(cv[:, :, t % 2, :], x2[:, t, :].rearrange("p (a b) -> p a b", a=2), ACT.Square,
                               accum_out=ss[:, t:t + 1]).then_inc(final_sq, 1)

        @block.vector
        def _(dve):
            steps = Steps(dve, dve_step)
            link, mark = steps.link, steps.mark

            def split_lo(n):
                dve.wait_ge(hi_ready, n + 1)
                dve.tensor_tensor(w_lo[:, n % 4, :], raw[:, n % 2, :], w_hi[:, n % 4, :].bitcast(F32),
                                  ALU.subtract).then_inc(lo_ready, 1)

            def rsqrt(sums, count, cols):
                v, y, t = var[:, 0:cols], rstd[:, 0:cols], newt[:, 0:cols]
                link(dve.tensor_scalar(v, sums, 1.0 / count, EPS, ALU.mult, ALU.add))
                link(dve.tensor_scalar(seed_i[:, 0:cols], v.bitcast(I32), 1, None, ALU.logical_shift_right))
                link(dve.tensor_scalar(y.bitcast(I32), seed_i[:, 0:cols], -1.0, float(0x5F3759DF), ALU.mult, ALU.add))
                for _ in range(3):
                    link(dve.scalar_tensor_tensor(t, y, -0.5, y, ALU.mult, ALU.mult))
                    link(dve.tensor_tensor(t, t, v, ALU.mult))
                    link(dve.scalar_tensor_tensor(y, t, 1.5, y, ALU.add, ALU.mult))

            def norm_diag(stage, first, count):
                dve.wait_ge(sumsq_ready, 4 * (stage - 1) + first + count)
                rsqrt(ss[:, first:first + count], D, count)
                for i in range(count):
                    dve.tensor_scalar(diag[:, first + i, :], ident[:, :], rstd[:, i:i + 1], None,
                                      ALU.mult).then_inc(diag_ready, 1)

            def norm_gain(stage, t):
                gT = g1T if stage == 1 else g2T
                for j in range(2):
                    tag = (f"norm{stage}", t, j)
                    wait_full(dve, tag)
                    if stage == 1 and t == 0 and j == 0:
                        dve.wait_ge(params_ready, 1)
                    dve.tensor_tensor(h32[:, t % 2, j, :, :], B(tag).rearrange("p (k t) -> p k t", k=4),
                                      gT[:, 4 * j:4 * j + 4].unsqueeze(2).to_broadcast([P, 4, P]),
                                      ALU.mult).then_inc(freesem(tag), 1)

            def norm_lo(stage, t):
                for j in range(2):
                    dve.wait_ge(h_hi_ready, 8 * (stage - 1) + 2 * t + j + 1)
                    sl = slice(t * P, (t + 1) * P)
                    dve.tensor_tensor(hT_lo[:, 4 * j:4 * j + 4, sl], h32[:, t % 2, j, :, :],
                                      hT_hi[:, 4 * j:4 * j + 4, sl].bitcast(F32), ALU.subtract).then_inc(hT_ready, 1)

            dve.wait_ge(consts, 1)
            norm_diag(1, 0, 1)
            dve.wait_ge(stage_T, 1)
            dve.tensor_copy(par_a[:, :], ps[:, 6, 0:96]).then_inc(params_ready, 1)
            norm_gain(1, 0)
            split_lo(0)
            norm_lo(1, 0)
            norm_diag(1, 1, 3)
            split_lo(1)
            norm_gain(1, 1)
            norm_lo(1, 1)
            norm_gain(1, 2)
            norm_lo(1, 2)
            dve.tensor_copy(par_b[:, :], ps[:, 6, 96:184]).then_inc(params_ready, 1)
            norm_gain(1, 3)
            norm_lo(1, 3)

            dve.wait_ge(wif_hi_ready, 1)
            dve.tensor_tensor(wif_lo[:, :, 0:4], wif_raw[:, :, 0:4], wif_hi[:, :, 0:4].bitcast(F32), ALU.subtract)
            dve.tensor_tensor(wif_lo[:, :, 32:36], wif_raw[:, :, 4:8], wif_hi[:, :, 32:36].bitcast(F32),
                              ALU.subtract).then_inc(wif_ready, 1)
            split_lo(2)
            split_lo(3)
            dve.wait_ge(trig_ready, 1)

            def rope(c):
                t, tag, b = c % NT, ("block", c), c % 2
                wait_full(dve, tag)
                src = B(tag).rearrange("p (h s c) -> p h s c", h=AH, s=2)
                m1 = rp[:, b, 0, :].rearrange("p (h s c) -> p h s c", h=AH, s=2)
                m2 = rp[:, b, 1, :].rearrange("p (h s c) -> p h s c", h=AH, s=2)
                cb = cosT[:, t, :].unsqueeze(1).to_broadcast([P, 2 * AH, 32])
                dve.tensor_tensor(rp[:, b, 0, :].rearrange("p (h c) -> p h c", c=32),
                                  B(tag).rearrange("p (h c) -> p h c", c=32), cb, ALU.mult)
                for s in range(2):
                    sb = sinT[:, t, s, :].unsqueeze(1).to_broadcast([P, AH, 32])
                    ins = dve.tensor_tensor(m2[:, :, s, :], src[:, :, 1 - s, :], sb, ALU.mult)
                ins.then_inc(freesem(tag), 1)
                wait_freed(dve, tag)
                if c >= 2:
                    wait_full(dve, ("rope", c - 2))
                dve.tensor_tensor(qr[:, b, :], rp[:, b, 0, :], rp[:, b, 1, :], ALU.add).then_inc(rope_done, 1)

            def if_rows():
                r = lambda k: rows[:, k, :]
                seg = lambda k, t: rows[:, k, t * P:(t + 1) * P]
                dve.wait_ge(f_row, 1)
                dve.scalar_tensor_tensor(r(1), r(0), -1.0, r(0), ALU.mult, ALU.max).then_inc(f_abs, 1)
                dve.wait_ge(f_ln, 1)
                link(dve.scalar_tensor_tensor(r(0), r(0), 0.0, r(1), ALU.min, ALU.subtract))
                for t in range(NT):
                    n = mark(dve.tensor_tensor_scan(seg(2, t), ones_r[:, :], seg(0, t), 0.0, ALU.mult, ALU.add))
                dve.wait_ge(dve_step, n)
                wait_freed(dve, ("gates_if",))
                for t in range(NT):
                    n = mark(dve.tensor_tensor(seg(4 + t, t), seg(3, t), seg(2, t), ALU.subtract))
                dve.wait_ge(dve_step, n)
                for t in range(NT):
                    total = rows[:, 2, t * P - 1:t * P] if t else None
                    if t:
                        link(dve.tensor_tensor(carry[:, t:t + 1], rows[:, 1, t * P - 1:t * P], total, ALU.add))
                        mark(dve.tensor_scalar(rows[:, 4 + t, 0:t * P], rows[:, 3 + t, 0:t * P], total, None, ALU.add))
                    link(dve.tensor_tensor_scan(seg(1, t), ones_r[:, :], seg(4 + t, t),
                                                carry[:, t:t + 1] if t else 0.0, ALU.mult, ALU.max))
                dve.tensor_scalar(neg_m[:, :], r(1), -1.0, None, ALU.mult)
                dve.scalar_tensor_tensor(r(0), r(1), -1.0, r(2), ALU.mult, ALU.subtract).then_inc(rows_ready, 1)

            def attn_max(g):
                n = (g // 4 + 1) * P
                wait_full(dve, ("score", g, 0))
                wait_full(dve, ("score", g, 1))
                dve.reduce_max(nmax[:, g % 2, :], ps[:, 2:4, 0:n], axis=AX_X, negate=True).then_inc(max_ready, 1)

            def attn_probT(g):
                n = (g // 4 + 1) * P
                wait_full(dve, ("probT", g, 1))
                if g >= 1:
                    dve.wait_ge(pv_done, g)
                dve.tensor_copy(probT[:, 1, 0:n], B(("probT", g, 1))[:, 0:n]).then_inc(freesem(("probT", g, 1)), 1)

            def attn_out(i):
                dve.wait_ge(pv_done, 4 * i + 4)
                wait_freed(dve, ("score", 4 * i + 3, 1))
                link(dve.reciprocal(rinv[:, :], rsum[:, i % 2, :]))
                tag = ("attn", i)
                if i >= 2:
                    wait_full(dve, ("attnT", i - 2))
                dve.tensor_tensor(tok_a[:, i % 2, :].rearrange("p (h d) -> p h d", h=AH),
                                  B(tag).rearrange("p (h d) -> p h d", h=AH),
                                  rinv[:, :].unsqueeze(2).to_broadcast([P, AH, AD]), ALU.mult).then_inc(freesem(tag), 1)

            def decay_mask(i):
                tag = ("decay", i)
                wait_full(dve, tag)
                if i:
                    dve.wait_ge(decay_ready, 4 * i)
                else:
                    dve.wait_ge(pv_done, 16)
                ins = dve.tensor_tensor(em[:, 0, :].rearrange("p (h t) -> p h t", h=MH),
                                        B(tag).rearrange("p (h t) -> p h t", h=MH),
                                        mask_st[:, :].unsqueeze(1).to_broadcast([P, MH, P]), ALU.add)
                ins.then_inc(em_ready if i else freesem(tag), 1)

            def mlstm_scores(g):
                i = g // 2
                n = (i + 1) * P
                for e in range(2):
                    tag = ("mscore", g, e)
                    wait_full(dve, tag)
                    dve.wait_ge(decay_ready, 2 * g + e + 1)
                    dve.scalar_tensor_tensor(prob[:, e, 0:n], B(tag)[:, 0:n], 0.25 * MD ** -0.5, prob[:, e, 0:n],
                                             ALU.mult, ALU.mult).then_inc(freesem(tag), 1)

            def mlstm_out(g):
                i, hp, tag = g // 2, g % 2, ("mnum", g)
                wait_full(dve, tag)
                num = B(tag)[:, 0:2 * (MD + 1)].rearrange("p (e d) -> p e d", e=2)
                if g == 0:
                    dve.wait_ge(expm_ready, 1)
                link(dve.tensor_scalar(dinv[:, :].unsqueeze(2), num[:, :, MD:MD + 1], -1.0, None, ALU.mult))
                link(dve.tensor_tensor(den[:, :].unsqueeze(2), num[:, :, MD:MD + 1], dinv[:, :].unsqueeze(2), ALU.max))
                link(dve.tensor_tensor(den[:, :], den[:, :], expm[:, 4 * i + 2 * hp:4 * i + 2 * hp + 2], ALU.max))
                link(dve.reciprocal(dinv[:, :], den[:, :]))
                if hp == 0 and i >= 1:
                    dve.wait_ge(hm_hi_ready, i)
                mark(dve.tensor_tensor(em[:, 1, 256 * hp:256 * hp + 256].rearrange("p (e d) -> p e d", e=2),
                                       num[:, :, 0:MD], dinv[:, :].unsqueeze(2).to_broadcast([P, 2, MD]), ALU.mult))
                dve.wait_ge(dve_step, steps.n)
                dve.nop().then_inc(freesem(tag), 1)
                dve.nop().then_inc(hm_raw, 1)

            def mlstm_norm(i):
                dve.wait_ge(hm_sq, 2 * i + 2)
                rsqrt(ss[:, 4:8], MD, 4)
                dve.wait_ge(o_ready, i + 1)
                for h in range(MH):
                    sl = slice(h * P, (h + 1) * P)
                    ins = dve.scalar_tensor_tensor(em[:, 1, sl], em[:, 1, sl], rstd[:, h:h + 1], o_sig[:, i, sl],
                                                   ALU.mult, ALU.mult)
                ins.then_inc(hm_ready, 1)

            def mlstm_gain(i):
                tag = ("mT", i)
                wait_full(dve, tag)
                dve.tensor_tensor(em[:, 1, :].rearrange("p (k t) -> p k t", k=4),
                                  B(tag).rearrange("p (k t) -> p k t", k=4),
                                  mgT.unsqueeze(2).to_broadcast([P, 4, P]), ALU.mult).then_inc(freesem(tag), 1)
                dve.wait_ge(hm_hi_ready, i + 1)
                sl = slice(i * P, (i + 1) * P)
                dve.tensor_tensor(hmT_lo[:, :, sl], em[:, 1, :].rearrange("p (k t) -> p k t", k=4),
                                  hmT_hi[:, :, sl].bitcast(F32), ALU.subtract).then_inc(hmT_ready, 1)

            for c in range(NBLK):
                tag = ("block", c)
                if c < 8:
                    rope(c)
                if c == 8:
                    if_rows()
                if 12 <= c < 20:
                    m = c - 12
                    a = cacc[:, m % 2, :]
                    dve.wait_ge(conv_tap, m + 1)
                    for sh in (1, 2, 3):
                        ins = dve.scalar_tensor_tensor(a[:, sh:], B(tag)[:, 0:SEQ - sh], tap_m(3 - sh, m), a[:, sh:],
                                                       ALU.mult, ALU.add)
                        if sh < 3:
                            link(ins)
                        else:
                            ins.then_inc(freesem(tag), 1)
                if c == 11:
                    wait_full(dve, ("cols_if",))
                    dve.tensor_copy(gcol[:, :], B(("cols_if",))[:, 0:56]).then_inc(freesem(("cols_if",)), 1)
                if 0 <= c - ATT < 16:
                    attn_max(c - ATT)
                if 0 <= c - ATT - 1 < 16:
                    attn_probT(c - ATT - 1)
                if 12 <= c < 20:
                    m = c - 12
                    dve.wait_ge(conv_tanh, m + 1)
                    dst = (qmT if m < 4 else kmT)[:, m % 4, :]
                    dve.scalar_tensor_tensor(dst, cth[:, m % 2, :], 1.0, cacc[:, m % 2, :], ALU.add,
                                             ALU.mult).then_inc(conv_done, 1)
                if 0 <= c - ATT - 5 <= 12 and (c - ATT - 5) % 4 == 0:
                    attn_out((c - ATT - 5) // 4)
                if 0 <= c - ATT - 6 <= 12 and (c - ATT - 6) % 4 == 0:
                    i = (c - ATT - 6) // 4
                    dve.wait_ge(at_hi_ready, i + 1)
                    sl = slice(i * P, (i + 1) * P)
                    dve.tensor_tensor(atT_lo[:, :, sl], B(("attnT", i)).rearrange("p (k t) -> p k t", k=4),
                                      atT_hi[:, :, sl].bitcast(F32), ALU.subtract).then_inc(freesem(("attnT", i)), 1)
                if 0 <= c - MLS < 8:
                    if (c - MLS) % 2 == 0:
                        decay_mask((c - MLS) // 2)
                    mlstm_scores(c - MLS)
                if 0 <= c - MLS - 3 <= 6 and (c - MLS - 3) % 2 == 0:
                    mlstm_gain((c - MLS - 3) // 2)
                if 0 <= c - MLS - 1 < 8:
                    mlstm_out(c - MLS - 1)
                    if (c - MLS - 1) % 2 == 1:
                        mlstm_norm((c - MLS - 1) // 2)
                if c % 4 == 3:
                    split_lo(2 * (c // 4) + 4)
                    split_lo(2 * (c // 4) + 5)

            def merge(n):
                ga = (gate_a0, gate_a1)[n // 4][:, n % 4, :]
                if n == 0:
                    wait_freed(dve, ("block", 39))
                if n == 4:
                    wait_freed(dve, ("gate", 3))
                for s, gt in ((0, ga), (1, gate_m[:, n % 4, :])):
                    tag = ("y", n, s)
                    wait_full(dve, tag)
                    dst = (prob, probT)[s][:, n % 2, :]
                    dve.scalar_tensor_tensor(dst, gt, 1.0, B(tag), ALU.add, ALU.mult).then_inc(freesem(tag), 1)
                wait_freed(dve, ("y", n, 0))
                wait_freed(dve, ("y", n, 1))
                dve.tensor_tensor(prob[:, n % 2, :], prob[:, n % 2, :], probT[:, n % 2, :], ALU.add).then_inc(m32_ready, 1)
                dve.wait_ge(mrg_hi_ready, n + 1)
                hi, lo = ((mrg_hi0, mrg_lo0), (mrg_hi1, mrg_lo1))[n // 4]
                dve.scalar_tensor_tensor(lo[:, n % 4, :], prob[:, n % 2, :], 0.5, hi[:, n % 4, :].bitcast(F32),
                                         ALU.mult, ALU.subtract).then_inc(mrg_ready, 1)

            for n in range(4):
                merge(n)
            split_lo(2 * U_B0 + 4)
            split_lo(2 * U_B0 + 5)
            split_lo(2 * U_GM1 + 4)
            split_lo(2 * U_GM1 + 5)
            for n in range(4, 7):
                merge(n)
            split_lo(2 * U_B1 + 4)
            merge(7)
            split_lo(2 * U_B1 + 5)

            def residual(t, n):
                if t == 0 and n == 0:
                    dve.wait_ge(x_again, 16)
                tag = ("out", t, n)
                wait_full(dve, tag)
                sl = x2[:, t, n * 512:(n + 1) * 512]
                dve.tensor_tensor(sl, B(tag), sl, ALU.add).then_inc(freesem(tag), 1)

            for t in range(NT - 1):
                residual(t, 0)
                residual(t, 1)
                norm_diag(2, t, 1)
                norm_gain(2, t)
                norm_lo(2, t)
            residual(3, 0)
            split_lo(2 * U_O0 + 4)
            residual(3, 1)
            norm_diag(2, 3, 1)
            split_lo(2 * U_O0 + 5)
            norm_gain(2, 3)
            norm_lo(2, 3)
            split_lo(2 * U_O1 + 4)
            split_lo(2 * U_O1 + 5)

            def glu(g, f, n, it, step):
                f0 = g * GROUP[0]
                banks = [plan[("up", f, s)] for s in range(2)]
                for sh in (1, 2):
                    for s in range(2):
                        a = cv[:, f % 2, s, :]
                        if sh == 1:
                            dve.wait_ge(glu_tap, 8 * it + (2 * f + s + 1))
                        else:
                            dve.wait_ge(dve_step, step + (s + 1))
                        ins = dve.scalar_tensor_tensor(a[:, sh:], ps[:, banks[s][0], 0:SEQ - sh],
                                                       tap_f(2 - sh, 4 * it + (f + NF * s)), a[:, sh:],
                                                       ALU.mult, ALU.add)
                        ins.then_inc(dve_step if sh == 1 else bank_free[banks[s][0]], 1)
                m = n + 4
                dve.wait_ge(hi_ready, 4 * it + (m + 1))
                dve.tensor_tensor(w_lo[:, m % 4, :], raw[:, m % 2, :], w_hi[:, m % 4, :].bitcast(F32),
                                  ALU.subtract).then_inc(lo_ready, 1)
                dve.wait_ge(glu_silu, 4 * it + (f + 1))
                dve.wait_ge(bank_free[banks[1][0]], 2 * it + (banks[1][1] + 1))
                dve.tensor_tensor(sil[:, f % 2, :], sil[:, f % 2, :], cv[:, f % 2, 1, :], ALU.mult).then_inc(glu_prod, 1)
                dve.wait_ge(glu_hi, 4 * it + (f + 1))
                sl = bass.ds(4 * it + (f - f0), 1)
                dve.tensor_tensor(act_lo[:, sl, :], sil[:, f % 2:f % 2 + 1, :], act_hi[:, sl, :].bitcast(F32),
                                  ALU.subtract).then_inc(act_ready, 1)

            for g in range(2):
                f0, n0 = g * GROUP[0], N_UP[g]
                first = 0
                if g == 0:
                    for j in range(4):
                        glu(g, f0 + j, n0 + j, 0, steps.n)
                        steps.n += 2
                    first = 4
                loops = (GROUP[g] - first) // 4
                with dve.Fori(0, loops) as it:
                    for j in range(4):
                        glu(g, f0 + first + j, n0 + first + j, it, 8 * it + (steps.n + 2 * j))
                steps.n += 8 * loops
                for j in range(first + 4 * loops, GROUP[g]):
                    glu(g, f0 + j, n0 + j, 0, steps.n)
                    steps.n += 2
                for d in range(GROUP[g] // 2 - 1):
                    if N_DOWN[g] + d + 4 < N_LOADS:
                        split_lo(N_DOWN[g] + d + 4)
                for t in range(NT):
                    for n in range(2):
                        tag = ("down", g, t, n)
                        wait_full(dve, tag)
                        sl = x2[:, t, n * 512:(n + 1) * 512]
                        if g == 1:
                            wait_freed(dve, ("down", 0, t, n))
                        else:
                            wait_freed(dve, ("out", t, n))
                        dve.tensor_tensor(sl, B(tag), sl, ALU.add).then_inc(freesem(tag), 1)
                    if g == 1:
                        dve.wait_ge(final_sq, t + 1)
                        rsqrt(ss[:, t:t + 1], D, 1)
                        if t == 0:
                            dve.wait_ge(gf_loaded, 16)
                        dve.scalar_tensor_tensor(out_sb[:, t, :], x2[:, t, :], rstd[:, 0:1], gF[:, :], ALU.mult,
                                                 ALU.mult).then_inc(out_ready, 1)
                if g == 0:
                    split_lo(N_DOWN[0] + GROUP[0] // 2 + 3)

        @block.tensor
        def _(pe):
            def mm3(dst, l_hi, l_lo, r_hi, r_lo, start, stop):
                pe.matmul(dst, l_hi, r_hi, start=start, stop=False)
                pe.matmul(dst, l_hi, r_lo, start=False, stop=False)
                return pe.matmul(dst, l_lo, r_hi, start=False, stop=stop)

            def wslice(n, cols):
                k = LOAD // cols
                return [w[:, n % 4, :].rearrange("p (k c) -> p k c", k=k) for w in (w_hi, w_lo)]

            def token_block(tag, u, t, src=None):
                wait_bank(pe, tag)
                for k in range(KT):
                    n = 2 * u + k // 4
                    if k % 4 == 0:
                        pe.wait_ge(lo_ready, n + 1)
                        if u == U_QA:
                            pe.wait_ge(hT_ready, 2 * t + k // 4 + 1)
                    elif u == U_O0 and t == 0:
                        pe.wait_ge(mrg_ready, k + 1)
                    wh, wl = wslice(n, 512)
                    if src is None:
                        sl = slice(t * P, (t + 1) * P)
                        lh, ll = hT_hi[:, k, sl], hT_lo[:, k, sl]
                    else:
                        lh, ll = src(k, t)
                    ins = mm3(B(tag), lh, ll, wh[:, k % 4, :], wl[:, k % 4, :], k == 0, k == KT - 1)
                ins.then_inc(fullsem(tag), 1)

            def feature_block(tag, u, m):
                wait_bank(pe, tag)
                for k in range(KT):
                    n = 2 * u + k // 4
                    if k % 4 == 0:
                        pe.wait_ge(lo_ready, n + 1)
                    wh, wl = wslice(n, 512)
                    sl = slice(m * P, (m + 1) * P)
                    ins = mm3(B(tag), wh[:, k % 4, sl], wl[:, k % 4, sl], hT_hi[:, k, :], hT_lo[:, k, :],
                              k == 0, k == KT - 1)
                ins.then_inc(fullsem(tag), 1)

            def norm_T(stage, t):
                src = x_sb if stage == 1 else x2
                pe.wait_ge(diag_ready, 4 * (stage - 1) + t + 1)
                for j in range(2):
                    tag = (f"norm{stage}", t, j)
                    wait_bank(pe, tag)
                    for k in range(4):
                        ins = pe.matmul(B(tag)[:, k * P:(k + 1) * P], src[:, t, (4 * j + k) * P:(4 * j + k + 1) * P],
                                        diag[:, t, :], start=True, stop=True)
                    ins.then_inc(fullsem(tag), 1)

            pe.wait_ge(consts, 1)
            pe.wait_ge(params_loaded, 32)
            pe.wait_ge(rest_loaded, 64)
            pe.transpose(ps[:, 6, 0:96], stg_a[:, :], ident[0:96, 0:96])
            pe.transpose(ps[:, 6, 96:184], stg_b[:, :], ident[0:88, 0:88]).then_inc(stage_T, 1)
            norm_T(1, 0)
            pe.wait_ge(consts, 2)

            def score(g):
                i, hp = g // 4, g % 4
                n = (i + 1) * P
                if g == 0:
                    wait_freed(pe, ("rope", 6))
                    wait_freed(pe, ("rope", 7))
                for e in range(2):
                    tag = ("score", g, e)
                    wait_bank(pe, tag)
                    rows64 = slice(64 * e, 64 * e + 64)
                    pe.matmul(B(tag)[:, 0:n], qT[rows64, hp, i * P:(i + 1) * P], kT[rows64, hp, 0:n],
                              start=True, stop=False)
                    pe.matmul(B(tag)[:, i * P:n], ident_b[:, :], mask_ts[:, :], start=False,
                              stop=True).then_inc(fullsem(tag), 1)

            def prob_T(g):
                i = g // 4
                for e in range(2):
                    tag = ("probT", g, e)
                    wait_bank(pe, tag)
                    wait_freed(pe, ("score", g, e))
                    for j in range(i + 1):
                        ins = pe.transpose(B(tag)[:, j * P:(j + 1) * P], prob[:, e, j * P:(j + 1) * P], ident[:, :])
                    ins.then_inc(fullsem(tag), 1)

            def prob_v(g):
                i, hp = g // 4, g % 4
                tag = ("attn", i)
                if hp == 0:
                    wait_bank(pe, tag)
                    wait_freed(pe, ("block", 8 + i))
                for e in range(2):
                    h = 2 * hp + e
                    wait_freed(pe, ("probT", g, e))
                    for j in range(i + 1):
                        ins = pe.matmul(B(tag)[:, h * AD:(h + 1) * AD], probT[:, e, j * P:(j + 1) * P],
                                        va[:, j, h * AD:(h + 1) * AD], start=(j == 0), stop=(j == i))
                ins.then_inc(pv_done, 1)

            def attn_T(i):
                tag = ("attnT", i)
                wait_bank(pe, tag)
                wait_freed(pe, ("attn", i))
                for k in range(4):
                    ins = pe.transpose(B(tag)[:, k * P:(k + 1) * P], tok_a[:, i % 2, k * P:(k + 1) * P], ident[:, :])
                ins.then_inc(fullsem(tag), 1)

            def m_score(g):
                i, hp = g // 2, g % 2
                if hp == 0:
                    tag = ("decay", i)
                    wait_bank(pe, tag)
                    for h in range(MH):
                        ins = pe.matmul(B(tag)[:, h * P:(h + 1) * P], ident[0:4, h:h + 1].to_broadcast([4, P]),
                                        neg_m[:, i * P:(i + 1) * P], start=True, stop=True)
                    ins.then_inc(fullsem(tag), 1)
                if g == 0:
                    pe.wait_ge(conv_done, 8)
                for e in range(2):
                    tag, h = ("mscore", g, e), 2 * hp + e
                    wait_bank(pe, tag)
                    for j in range(i + 1):
                        ins = pe.matmul(B(tag)[:, j * P:(j + 1) * P], kmT[:, h, j * P:(j + 1) * P],
                                        qmT[:, h, i * P:(i + 1) * P], start=True, stop=True)
                    ins.then_inc(fullsem(tag), 1)

            def m_num(g):
                i, hp, tag = g // 2, g % 2, ("mnum", g)
                wait_bank(pe, tag)
                if g == 0:
                    pe.wait_ge(ones_col, 1)
                    wait_freed(pe, ("block", 22))
                    wait_freed(pe, ("block", 23))
                for e in range(2):
                    h = 2 * hp + e
                    wait_freed(pe, ("mscore", g, e))
                    for j in range(i + 1):
                        ins = pe.matmul(B(tag)[:, e * (MD + 1):(e + 1) * (MD + 1)], prob[:, e, j * P:(j + 1) * P],
                                        vm[:, j, h, :], start=(j == 0), stop=(j == i))
                ins.then_inc(fullsem(tag), 1)

            def m_T(i):
                tag = ("mT", i)
                wait_bank(pe, tag)
                pe.wait_ge(hm_ready, i + 1)
                for k in range(4):
                    ins = pe.transpose(B(tag)[:, k * P:(k + 1) * P], em[:, 1, k * P:(k + 1) * P], ident[:, :])
                ins.then_inc(fullsem(tag), 1)

            for c in range(NBLK):
                u, m = c // 4, c % 4
                tag = ("block", c)
                if c < 2:
                    for t in ((), (1, 2))[c]:
                        norm_T(1, t)
                if u in (U_QM, U_KM, U_GA0, U_GM0, U_GA1):
                    feature_block(tag, u, m)
                else:
                    token_block(tag, u, m)
                if c == 1:
                    norm_T(1, 3)
                if 1 <= c <= 8:
                    rt = ("rope", c - 1)
                    wait_bank(pe, rt)
                    if c == 1:
                        pe.wait_ge(params_ready, 2)
                    pe.wait_ge(rope_done, c)
                    for k in range(4):
                        ins = pe.transpose(B(rt)[:, k * P:(k + 1) * P], qr[:, (c - 1) % 2, k * P:(k + 1) * P], ident[:, :])
                    ins.then_inc(fullsem(rt), 1)
                if c == 5:
                    gi = ("gates_if",)
                    wait_bank(pe, gi)
                    pe.wait_ge(wif_ready, 1)
                    for k in range(KT):
                        ins = mm3(B(gi), wif_hi[:, k, :], wif_lo[:, k, :], hT_hi[:, k, :], hT_lo[:, k, :],
                                  k == 0, k == KT - 1)
                    ins.then_inc(fullsem(gi), 1)
                if c == 11:
                    ci = ("cols_if",)
                    wait_bank(pe, ci)
                    pe.wait_ge(rows_ready, 1)
                    at = 0
                    for i in range(NT):
                        for j in range(i + 1):
                            pe.transpose(B(ci)[:, at:at + 4], rows[:, 4 + i, j * P:(j + 1) * P], ident[0:4, 0:4])
                            at += 4
                    for i in range(NT):
                        ins = pe.transpose(B(ci)[:, at:at + 4], rows[:, 0, i * P:(i + 1) * P], ident[0:4, 0:4])
                        at += 4
                    ins.then_inc(fullsem(ci), 1)
                if 0 <= c - ATT < 16:
                    score(c - ATT)
                if 0 <= c - ATT - 1 < 16:
                    prob_T(c - ATT - 1)
                if 0 <= c - ATT - 2 < 16:
                    prob_v(c - ATT - 2)
                if 0 <= c - ATT - 6 <= 12 and (c - ATT - 6) % 4 == 0:
                    attn_T((c - ATT - 6) // 4)
                if 0 <= c - MLS < 8:
                    m_score(c - MLS)
                if 0 <= c - MLS - 3 <= 6 and (c - MLS - 3) % 2 == 0:
                    m_T((c - MLS - 3) // 2)
                if 0 <= c - MLS - 1 < 8:
                    m_num(c - MLS - 1)

            def branches(u, n):
                m = n % 4
                for s, (src_hi, src_lo) in enumerate(((atT_hi, atT_lo), (hmT_hi, hmT_lo))):
                    tag = ("y", n, s)
                    wait_bank(pe, tag)
                    if n == 0:
                        if s == 0:
                            wait_freed(pe, ("attnT", 3))
                        else:
                            pe.wait_ge(hmT_ready, 4)
                    pe.wait_ge(lo_ready, 2 * u + s + 1)
                    wh, wl = wslice(2 * u + s, 512)
                    sl = slice(m * P, (m + 1) * P)
                    for k in range(4):
                        ins = mm3(B(tag), wh[:, k, sl], wl[:, k, sl], src_hi[:, k, :], src_lo[:, k, :], k == 0, k == 3)
                    ins.then_inc(fullsem(tag), 1)

            for n in range(4):
                branches(U_B0, n)
            for m in range(4):
                feature_block(("gate", m), U_GM1, m)
            for n in range(4, 8):
                branches(U_B1, n)

            def merged(k, t):
                hi, lo = ((mrg_hi0, mrg_lo0), (mrg_hi1, mrg_lo1))[k // 4]
                sl = slice(t * P, (t + 1) * P)
                return hi[:, k % 4, sl], lo[:, k % 4, sl]

            pe.wait_ge(mrg_ready, 5)
            for t in range(NT):
                for n in range(2):
                    token_block(("out", t, n), U_O0 + n, t, merged)
                    if n == 0 and t >= 1:
                        norm_T(2, t - 1)
            def up(f, n, it):
                pe.wait_ge(lo_ready, 4 * it + (n + 1))
                for s in range(2):
                    bank, k0, _ = plan[("up", f, s)]
                    pe.wait_ge(bank_free[bank], 2 * it + k0)
                    wh, wl = [w[:, n % 4, s * 1024:(s + 1) * 1024].rearrange("p (k c) -> p k c", k=KT) for w in (w_hi, w_lo)]
                    for k in range(KT):
                        ins = mm3(ps[:, bank, :], wh[:, k, :], wl[:, k, :], hT_hi[:, k, :], hT_lo[:, k, :],
                                  k == 0, k == KT - 1)
                    ins.then_inc(bank_full[bank], 1)

            def up_first():
                n = N_UP[0]
                pe.wait_ge(lo_ready, n + 1)
                for part in range(2):
                    cols = (slice(0, 3 * P), slice(3 * P, SEQ))[part]
                    if part == 0:
                        pe.wait_ge(hT_ready, 14)
                    else:
                        pe.wait_ge(hT_ready, 16)
                    for s in range(2):
                        tag = ("up", 0, s)
                        if part == 0:
                            wait_bank(pe, tag)
                        wh, wl = [w[:, n % 4, s * 1024:(s + 1) * 1024].rearrange("p (k c) -> p k c", k=KT) for w in (w_hi, w_lo)]
                        for k in range(KT):
                            ins = mm3(B(tag)[:, cols], wh[:, k, :], wl[:, k, :], hT_hi[:, k, cols], hT_lo[:, k, cols],
                                      k == 0, k == KT - 1)
                            if part == 0 and s == 0 and k == KT - 1:
                                norm_T(2, NT - 1)
                        if part == 1:
                            ins.then_inc(fullsem(tag), 1)

            up_first()
            for g in range(2):
                f0, n0 = g * GROUP[0], N_UP[g]
                first = 0
                if g == 0:
                    for j in range(1, 4):
                        up(f0 + j, n0 + j, 0)
                    first = 4
                loops = (GROUP[g] - first) // 4
                with pe.Fori(0, loops) as it:
                    for j in range(4):
                        up(f0 + first + j, n0 + first + j, it)
                for j in range(first + 4 * loops, GROUP[g]):
                    up(f0 + j, n0 + j, 0)
                nd = GROUP[g] // 2

                def down(d, t, c):
                    tag, n = ("down", g, t, c), N_DOWN[g] + d
                    if d == 0:
                        wait_bank(pe, tag)
                    wh, wl = wslice(n, 1024)
                    sl, cs = slice(t * P, (t + 1) * P), slice(c * 512, (c + 1) * 512)
                    for k in range(2):
                        ins = mm3(B(tag), act_hi[:, 2 * d + k, sl], act_lo[:, 2 * d + k, sl], wh[:, k, cs], wl[:, k, cs],
                                  d == 0 and k == 0, d == nd - 1 and k == 1)
                    if d == nd - 1:
                        ins.then_inc(fullsem(tag), 1)
                    return ins

                together = nd - 1 if g == 0 else nd - 2
                for d in range(together):
                    pe.wait_ge(lo_ready, N_DOWN[g] + d + 1)
                    pe.wait_ge(act_ready, f0 + 2 * d + 2)
                    for t in (2, 3, 0, 1) if d == 0 else range(NT):
                        for c in range(2):
                            ins = down(d, t, c)
                    ins.then_inc(down_used, 1)
                pe.wait_ge(lo_ready, N_DOWN[g] + nd)
                pe.wait_ge(act_ready, f0 + 2 * nd)
                for t in range(NT):
                    for c in range(2):
                        for d in range(together, nd):
                            down(d, t, c)


_INS = ["x", "positions", "norm_mix_g", "w_in", "conv_mlstm", "i_bias", "f_bias", "mlstm_norm_g", "w_branch_attn",
        "w_branch_mlstm", "w_out", "norm_ffn_g", "w_up", "conv_ffn", "w_down", "norm_final_g"]


def kernel(**inputs):
    import numpy as _np
    import concourse.bacc as _bacc
    from concourse import mybir as _mybir
    from concourse.bass_utils import run_bass_kernel_spmd as _run

    nc = _bacc.Bacc("TRN2", target_bir_lowering=False, num_devices=1)
    arrays, args = {}, []
    for name in _INS:
        a = _np.ascontiguousarray(inputs[name])
        arrays[f"in_{name}"] = a
        args.append(nc.dram_tensor(f"in_{name}", a.shape, _mybir.dt.from_np(a.dtype), kind="ExternalInput").ap())
    freq = (10000.0 ** (-_np.arange(32) / 32.0)).astype(_np.float32)[None]
    arrays["inv_freq"] = freq
    args.append(nc.dram_tensor("inv_freq", freq.shape, _mybir.dt.float32, kind="ExternalInput").ap())
    args.append(nc.dram_tensor("out_0", (1, SEQ, D), _mybir.dt.float32, kind="ExternalOutput").ap())
    build(nc, *args)
    r = _run(nc, [arrays], core_ids=[0])
    return r.results[0]["out_0"]
```

```python
from contextlib import ExitStack

import numpy as np

import concourse.bass as bass
from concourse import mybir

P = 128
F32 = mybir.dt.float32
F32R = mybir.dt.float32r
BF16 = mybir.dt.bfloat16
I32 = mybir.dt.int32
ALU = mybir.AluOpType
ACT = mybir.ActivationFunctionType
AX_X = mybir.AxisListType.X

SEQ, D = 512, 1024
NT = SEQ // P
KT = D // P
AH, AD = 8, 64
MH, MD = 4, 128
BW = 512
FF = 2816
NF = FF // P
GROUP = (12, 10)
EPS = 1e-6
NEG = -1e30
COL_IF = 7 * BW
COL_GA = COL_IF + 2 * MH
COL_GM = COL_GA + D
LOAD = 2048
TWO_PI = 6.283185307179586
ROUND = 1.5 * 2.0 ** 23

U_QA, U_KA, U_VA, U_QM, U_KM, U_VM, U_OM, U_GA0, U_GM0, U_GA1, U_B0, U_GM1, U_B1, U_O0, U_O1 = range(15)
N_UP = (2 * (U_O1 + 1), 2 * (U_O1 + 1) + GROUP[0] + GROUP[0] // 2)
N_DOWN = (N_UP[0] + GROUP[0], N_UP[1] + GROUP[1])
N_LOADS = N_DOWN[1] + GROUP[1] // 2
NBLK = 40
ATT = 10
MLS = 27


def split_12bit(value, parts):
    out = []
    for _ in range(parts):
        e = int(np.floor(np.log2(abs(value)))) - 11
        q = round(value / 2.0 ** e) * 2.0 ** e
        out.append(q)
        value -= q
    return out


class BankPlan:

    def __init__(self):
        self.at, self.uses, self.fulls = {}, [0] * 8, [0] * 8

    def use(self, tag, bank, signals_full=True):
        self.fulls[bank] += signals_full
        self.at[tag] = (bank, self.uses[bank], self.fulls[bank])
        self.uses[bank] += 1


def plan_banks():
    plan = BankPlan()
    for t in range(NT):
        for j in range(2):
            plan.use(("norm1", t, j), (2 if t % 2 == 0 else 4) + j)
    for c in range(NBLK):
        plan.use(("block", c), c % 2)
        if 2 <= c <= 9:
            plan.use(("rope", c - 2), 6 + c % 2)
        if c == 5:
            plan.use(("gates_if",), 4)
        if c == 11:
            plan.use(("cols_if",), 7)
        if 0 <= c - ATT < 16:
            for e in range(2):
                plan.use(("score", c - ATT, e), 2 + e)
        if 0 <= c - ATT - 1 < 16:
            for e in range(2):
                plan.use(("probT", c - ATT - 1, e), 4 + e)
        if 0 <= c - ATT - 2 < 16 and (c - ATT - 2) % 4 == 0:
            plan.use(("attn", (c - ATT - 2) // 4), 6, signals_full=False)
        if 0 <= c - ATT - 6 <= 12 and (c - ATT - 6) % 4 == 0:
            plan.use(("attnT", (c - ATT - 6) // 4), 7)
        if 0 <= c - MLS < 8:
            if (c - MLS) % 2 == 0:
                plan.use(("decay", (c - MLS) // 2), 6)
            for e in range(2):
                plan.use(("mscore", c - MLS, e), 2 + e)
        if 0 <= c - MLS - 1 < 8:
            plan.use(("mnum", c - MLS - 1), 4 + (c - MLS - 1) % 2)
        if 0 <= c - MLS - 4 <= 6 and (c - MLS - 4) % 2 == 0:
            plan.use(("mT", (c - MLS - 4) // 2), 7)
    ring = 0

    def ring_use(tag):
        nonlocal ring
        plan.use(tag, ring % 4)
        ring += 1

    for n in range(4):
        ring_use(("y", n, 0))
        ring_use(("y", n, 1))
    for m in range(4):
        ring_use(("gate", m))
    for n in range(4, 8):
        ring_use(("y", n, 0))
        ring_use(("y", n, 1))
    for t in range(NT):
        for n in range(2):
            ring_use(("out", t, n))
    for t in range(NT):
        for j in range(2):
            plan.use(("norm2", t, j), (4 if t % 2 == 0 else 6) + j)
    for g in range(2):
        first = g * GROUP[0]
        for f in range(first, first + GROUP[g]):
            ring_use(("up", f, 0))
            ring_use(("up", f, 1))
        for t in range(NT):
            for n in range(2):
                plan.use(("down", g, t, n), 2 * t + n)
    return plan


def build(nc, x, positions, norm_mix_g, w_in, conv_mlstm, i_bias, f_bias, mlstm_norm_g, w_branch_attn,
          w_branch_mlstm, w_out, norm_ffn_g, w_up, conv_ffn, w_down, norm_final_g, inv_freq, out):
    plan = plan_banks().at
    x_v = x.rearrange("b (t p) d -> p (b t) d", p=P)
    out_v = out.rearrange("b (t p) d -> p (b t) d", p=P)
    w_in2 = w_in[0].rearrange("(k p) c -> p k c", p=P)
    w_out2 = w_out[0].rearrange("(k p) c -> p k c", p=P)
    w_ba = w_branch_attn[0].rearrange("(k p) c -> p k c", p=P)
    w_bm = w_branch_mlstm[0].rearrange("(k p) c -> p k c", p=P)
    w_up2 = w_up[0].rearrange("(k p) c -> p k c", p=P)
    w_dn = w_down[0].rearrange("(k p) c -> p k c", p=P)

    ctx = ExitStack()
    with ctx:
        base = [-(-nc.sbuf_base // 64) * 64]
        ctx.enter_context(nc.sbuf_tensor("arena", [P, (nc.sbuf_usable_end - base[0] - 64) // 4], F32))

        def region(nbytes):
            at = base[0]
            base[0] += -(-nbytes // 32) * 32
            assert base[0] <= nc.sbuf_usable_end - 32, base
            return at

        def place(name, shape, dt, at):
            return nc.alloc_sbuf_tensor_at(name, shape, dt, offset=at)

        raw = place("w_raw", [P, 2, LOAD], F32, region(16384))
        w_hi = place("w_hi", [P, 4, LOAD], F32R, region(32768))
        w_lo = place("w_lo", [P, 4, LOAD], F32R, region(32768))
        at_h = region(32768)
        hT_hi = place("hT_hi", [P, KT, SEQ], F32R, at_h)
        hT_lo = place("hT_lo", [P, KT, SEQ], F32R, at_h + 16384)
        out_sb = place("out_sb", [P, NT, D], F32, at_h)
        gF = place("gF", [P, D], F32, at_h + 16384)
        at_x = region(16384)
        x_sb = place("x_sb", [P, NT, D], F32, at_x)
        rows = place("rows", [4, 8, SEQ], F32, at_x)
        o_sig = place("o_sig", [P, NT, BW], F32, at_x)
        tok_a = place("tok_a", [P, 2, BW], F32, at_x + 8192)
        gate_m = place("gate_m", [P, 4, SEQ], F32, at_x + 8192)
        mrg_lo1 = place("mrg_lo1", [P, 4, SEQ], F32R, at_x)
        cv = place("cv", [P, 2, 2, SEQ], F32, at_x)
        sil = place("sil", [P, 2, SEQ], F32, at_x + 8192)
        at_a = region(16384)
        kT_hi = place("kT_hi", [P, 4, SEQ], F32R, at_a)
        kT_lo = place("kT_lo", [P, 4, SEQ], F32R, at_a + 8192)
        hmT_hi = place("hmT_hi", [P, 4, SEQ], F32R, at_a)
        hmT_lo = place("hmT_lo", [P, 4, SEQ], F32R, at_a + 8192)
        x2 = place("x2", [P, NT, D], F32, at_a)
        at_b = region(16384)
        xs = place("xs", [P, 2, D], F32, at_b)
        sq1 = place("sq1", [P, NT, D], F32, at_a)
        h32 = place("h32", [P, 2, 2, 4, P], F32, at_b + 8192)
        qT_hi = place("qT_hi", [P, 4, SEQ], F32R, at_b)
        qT_lo = place("qT_lo", [P, 4, SEQ], F32R, at_b + 8192)
        atT_hi = place("atT_hi", [P, 4, SEQ], F32R, at_b)
        atT_lo = place("atT_lo", [P, 4, SEQ], F32R, at_b + 8192)
        at_c = region(16384)
        rp = place("rp", [P, 2, 2, BW], F32, at_c)
        qr = place("qr", [P, 2, BW], F32, at_c + 8192)
        cosT = place("cosT", [P, NT, 32], F32, at_c + 12288)
        sinT = place("sinT", [P, NT, 2, 32], F32, at_c + 12800)
        qmT = place("qmT", [P, 4, SEQ], F32, at_c)
        kmT = place("kmT", [P, 4, SEQ], F32, at_c + 8192)
        mrg_hi0 = place("mrg_hi0", [P, 4, SEQ], F32R, at_c)
        mrg_lo0 = place("mrg_lo0", [P, 4, SEQ], F32R, at_c + 8192)
        at_d = region(8192)
        trig = place("trig", [P, 7, P], F32, at_d)
        acc, cos_turns, sin_turns = trig[:, 0, :], trig[:, 1, :], trig[:, 4, :]
        va = place("va", [P, NT, BW], F32, at_d)
        gate_a0 = place("gate_a0", [P, 4, SEQ], F32, at_d)
        mrg_hi1 = place("mrg_hi1", [P, 4, SEQ], F32R, at_d)
        at_e = region(NT * MH * (MD + 1) * 4)
        wif_hi = place("wif_hi", [P, KT, P], F32R, at_e)
        wif_lo = place("wif_lo", [P, KT, P], F32R, at_e + 4096)
        cacc = place("cacc", [P, 2, SEQ], F32, at_e)
        cth = place("cth", [P, 2, SEQ], F32, at_e + 4096)
        vm = place("vm", [P, NT, MH, MD + 1], F32, at_e)
        gate_a1 = place("gate_a1", [P, 4, SEQ], F32, at_e)
        act_hi = place("act_hi", [P, GROUP[0], SEQ], F32R, at_b)
        act_lo = place("act_lo", [P, GROUP[0], SEQ], F32R, at_b + GROUP[0] * SEQ * 4)
        assert at_b + 2 * GROUP[0] * SEQ * 4 <= at_e + 8256

        def small(name, shape, dt):
            n = 4 if dt != BF16 else 2
            for s in shape[1:]:
                n *= s
            return place(name, shape, dt, region(n))

        at_p = base[0]
        prob = small("prob", [P, 2, SEQ], F32)
        wif_raw = place("wif_raw", [P, KT, 8], F32, at_p)
        pos_i = place("pos_i", [P, NT], I32, at_p + 256)
        pos_f = place("pos_f", [P, NT], F32, at_p + 288)
        invf = place("invf", [P, 32], F32, at_p + 320)
        ones_r = place("ones_r", [4, P], F32, at_p + 512)
        probT = small("probT", [P, 2, SEQ], F32)
        em = probT
        ident = small("ident", [P, P], F32)
        ident_b = small("ident_b", [P, P], BF16)
        mask_ts = small("mask_ts", [P, P], BF16)
        mask_st = small("mask_st", [P, P], F32)
        neg_m = small("neg_m", [36, SEQ], F32R)
        pick = small("pick", [36, MH], F32R)
        gcol = small("gcol", [P, 56], F32)
        expm = small("expm", [P, 16], F32)
        par_a = small("par_a", [P, 96], F32)
        par_b = small("par_b", [P, 88], F32)
        stg_a = place("stg_a", [96, P], F32, at_d + 4096)
        stg_b = place("stg_b", [88, P], F32, at_d + 4608)
        bias_if = small("bias_if", [36, 1], F32)
        ss = small("ss", [P, 16], F32)
        var = small("var", [P, 4], F32)
        seed_i = small("seed_i", [P, 4], I32)
        rstd = small("rstd", [P, 4], F32)
        newt = small("newt", [P, 4], F32)
        root = small("root", [P, 16], F32)
        eps = small("eps", [P, 1], F32)
        nmax = small("nmax", [P, 2, 2], F32)
        rsum = small("rsum", [P, 2, AH], F32)
        rinv = small("rinv", [P, AH], F32)
        den = small("den", [P, 2], F32)
        dinv = small("dinv", [P, 2], F32)
        carry = small("carry", [4, NT], F32)
        junk = small("junk", [P, 2, P], BF16)
        h_odd = small("h_odd", [P, BW], F32)

        def h_tok(i):
            return (em[:, 1, :], h_odd[:, :])[i % 2]

        g1T, g2T = par_a[:, 0:8], par_a[:, 8:16]
        mgT = par_a[:, 48:52]

        def tap_m(j, c):
            return par_a[:, 16 + 8 * j + c:17 + 8 * j + c]

        def tap_f(j, c):
            if j == 2:
                return par_a[:, bass.ds(52 + c, 1)]
            return par_b[:, bass.ds(2 * NF * j + c, 1)]

        ps = ctx.enter_context(nc.psum_tensor("ps", [P, 8, 512], F32))

        def sem(name):
            return ctx.enter_context(nc.semaphore(name))

        bank_full = [sem(f"bank_full{b}") for b in range(8)]
        bank_free = [sem(f"bank_free{b}") for b in range(8)]
        raw_loaded = [sem(f"raw_loaded{i}") for i in range(2)]
        hi_ready, lo_ready = sem("hi_ready"), sem("lo_ready")
        first_hi, first_lo = sem("first_hi"), sem("first_lo")
        x_loaded = [sem(f"x_loaded{t}") for t in range(NT)]
        x_again = sem("x_again")
        params_loaded, conv_loaded = sem("params_loaded"), sem("conv_loaded")
        pos_loaded, bias_loaded, wif_loaded = sem("pos_loaded"), sem("bias_loaded"), sem("wif_loaded")
        gf_loaded, out_stored = sem("gf_loaded"), sem("out_stored")
        consts, neg_m_zeroed = sem("consts"), sem("neg_m_zeroed")
        wif_zeroed, wif_hi_ready, wif_ready = sem("wif_zeroed"), sem("wif_hi_ready"), sem("wif_ready")
        stage_T, params_ready = sem("stage_T"), sem("params_ready")
        root_ready, eps_ready, rstd_ready = sem("root_ready"), sem("eps_ready"), sem("rstd_ready")
        sumsq_ready, xs_ready, h_hi_ready, hT_ready = sem("sumsq_ready"), sem("xs_ready"), sem("h_hi_ready"), sem("hT_ready")
        turns_ready, angles_ready, trig_ready = sem("turns_ready"), sem("angles_ready"), sem("trig_ready")
        rope_done, qk_hi_ready = sem("rope_done"), sem("qk_hi_ready")
        f_row, f_abs, f_ln, rows_ready, expm_ready = sem("f_row"), sem("f_abs"), sem("f_ln"), sem("rows_ready"), sem("expm_ready")
        max_ready, pv_done, at_hi_ready = sem("max_ready"), sem("pv_done"), sem("at_hi_ready")
        conv_tap, conv_tanh, conv_done = sem("conv_tap"), sem("conv_tanh"), sem("conv_done")
        ones_col = sem("ones_col")
        o_ready = sem("o_ready")
        em_ready, decay_ready, hm_raw, hm_sq, hm_ready = (
            sem("em_ready"), sem("decay_ready"), sem("hm_raw"), sem("hm_sq"), sem("hm_ready"))
        hm_hi_ready, hmT_ready = sem("hm_hi_ready"), sem("hmT_ready")
        m32_ready, mrg_hi_ready, mrg_ready = sem("m32_ready"), sem("mrg_hi_ready"), sem("mrg_ready")
        glu_tap, glu_silu, glu_prod, glu_hi, act_ready = (
            sem("glu_tap"), sem("glu_silu"), sem("glu_prod"), sem("glu_hi"), sem("act_ready"))
        down_used = sem("down_used")
        final_sq, final_sum, out_ready = sem("final_sq"), sem("final_sum"), sem("out_ready")
        last_gain, last_rstd, last_ready = sem("last_gain"), sem("last_rstd"), sem("last_ready")
        dve_step, act_step, pool_step = sem("dve_step"), sem("act_step"), sem("pool_step")

        def wait_full(eng, tag):
            bank, _, full = plan[tag]
            eng.wait_ge(bank_full[bank], full)

        def wait_freed(eng, tag):
            bank, k, _ = plan[tag]
            eng.wait_ge(bank_free[bank], k + 1)

        def wait_bank(eng, tag):
            bank, k, _ = plan[tag]
            if k:
                eng.wait_ge(bank_free[bank], k)

        def B(tag):
            return ps[:, plan[tag][0], :]

        def fullsem(tag):
            return bank_full[plan[tag][0]]

        def freesem(tag):
            return bank_free[plan[tag][0]]

        class Steps:

            def __init__(self, eng, s):
                self.eng, self.s, self.n = eng, s, 0

            def mark(self, ins):
                ins.then_inc(self.s, 1)
                self.n = self.n + 1
                return self.n

            def link(self, ins):
                self.eng.wait_ge(self.s, self.mark(ins))

        UNIT_LAST = {}
        for u in range(U_GA1 + 1):
            UNIT_LAST[u] = ("block", 4 * u + 3)
        UNIT_LAST[U_B0], UNIT_LAST[U_GM1], UNIT_LAST[U_B1] = ("y", 3, 1), ("gate", 3), ("y", 7, 1)
        UNIT_LAST[U_O0], UNIT_LAST[U_O1] = ("out", 3, 0), ("out", 3, 1)

        def wait_slot(eng, n):
            m = n - 4
            if m < 0:
                return
            if m in (2 * U_B0, 2 * U_B1):
                wait_full(eng, ("y", 3 if m == 2 * U_B0 else 7, 0))
                return
            if m < N_UP[0]:
                wait_full(eng, UNIT_LAST[m // 2])
                return
            for g in range(2):
                if N_UP[g] <= m < N_DOWN[g]:
                    wait_full(eng, ("up", g * GROUP[0] + m - N_UP[g], 1))
                    return
                last = N_DOWN[g] + GROUP[g] // 2 - 1
                if N_DOWN[g] <= m < last:
                    eng.wait_ge(down_used, (GROUP[0] // 2 - 1) * g + m - N_DOWN[g] + 1)
                    return
                if m == last:
                    wait_full(eng, ("down", g, 3, 1))
                    return

        block = ctx.enter_context(nc.Block())

        @block.sync
        def _(sp):
            def load(n, parts, wait=True):
                if n >= 2 and wait:
                    sp.wait_ge(lo_ready, n - 1)
                for k, (src, shape) in enumerate(parts):
                    dst = raw[:, n % 2, k * 1024:(k + 1) * 1024].rearrange("p (k c) -> p k c", k=shape)
                    sp.dma_start(dst, src).then_inc(raw_loaded[n % 2], 16)

            def rect(w, k0, c0, cols):
                k = 1024 // cols
                return [(w[:, k0 + i * k:k0 + (i + 1) * k, c0:c0 + cols], k) for i in range(2)]

            def unit(u, w, c0):
                for half in range(2):
                    load(2 * u + half, rect(w, 4 * half, c0, BW))

            sp.dma_start(x_sb[:, 0, :], x_v[:, 0, :]).then_inc(x_loaded[0], 16)
            load(0, rect(w_in2, 0, 0, BW))
            sp.dma_start(stg_a[16:48, :], conv_mlstm[0].rearrange("j (c p) -> (j c) p", p=P)).then_inc(params_loaded, 16)
            sp.dma_start(stg_a[48:52, :], mlstm_norm_g[0].rearrange("(k p) -> k p", p=P)).then_inc(params_loaded, 16)
            sp.dma_start(stg_a[52:96, :], conv_ffn[0, 2].rearrange("(c p) -> c p", p=P)).then_inc(params_loaded, 16)
            for t in range(1, NT):
                sp.dma_start(x_sb[:, t, :], x_v[:, t, :]).then_inc(x_loaded[t], 16)
                if t == 1:
                    load(1, rect(w_in2, 4, 0, BW))
            with sp.Fori(0, U_OM - U_KA + 1) as it:
                for half in range(2):
                    sp.wait_ge(lo_ready, 2 * it + (2 * U_KA + half - 1))
                    for i in range(2):
                        k0 = 4 * half + 2 * i
                        dst = raw[:, half, i * 1024:(i + 1) * 1024].rearrange("p (k c) -> p k c", k=2)
                        sp.dma_start(dst, w_in2[:, k0:k0 + 2, bass.ds(BW * it + U_KA * BW, BW)]).then_inc(
                            raw_loaded[half], 16)
            unit(U_GA0, w_in2, COL_GA)
            unit(U_GM0, w_in2, COL_GM)
            unit(U_GA1, w_in2, COL_GA + BW)
            load(2 * U_B0, rect(w_ba, 0, 0, BW))
            load(2 * U_B0 + 1, rect(w_bm, 0, 0, BW))
            unit(U_GM1, w_in2, COL_GM + BW)
            load(2 * U_B1, rect(w_ba, 0, BW, BW))
            load(2 * U_B1 + 1, rect(w_bm, 0, BW, BW))
            unit(U_O0, w_out2, 0)
            unit(U_O1, w_out2, BW)
            for g in range(2):
                with sp.Fori(0, GROUP[g] // 2) as it:
                    for j in range(2):
                        n = N_UP[g] + j
                        sp.wait_ge(lo_ready, 2 * it + (n - 1))
                        col = (2 * it + (g * GROUP[0] + j)) * P
                        for s in range(2):
                            dst = raw[:, n % 2, s * 1024:(s + 1) * 1024].rearrange("p (k c) -> p k c", k=KT)
                            sp.dma_start(dst, w_up2[:, :, bass.ds(col + s * FF, P)]).then_inc(raw_loaded[n % 2], 16)
                for d in range(GROUP[g] // 2):
                    k0 = g * GROUP[0] + 2 * d
                    load(N_DOWN[g] + d, [(w_dn[:, k0 + i:k0 + i + 1, :], 1) for i in range(2)])
            for t in range(NT - 1):
                sp.wait_ge(out_ready, t + 1)
                sp.dma_start(out_v[:, t, :], out_sb[:, t, :]).then_inc(out_stored, 16)
            sp.wait_ge(out_ready, NT)
            sp.dma_start(out_v[:, NT - 1, 512:], out_sb[:, NT - 1, 512:]).then_inc(out_stored, 16)
            sp.wait_ge(last_ready, 1)
            sp.dma_start(out_v[:, NT - 1, 0:512], out_sb[:, NT - 1, 0:512]).then_inc(out_stored, 16)
            sp.wait_ge(out_stored, 16 * (NT + 1))

        @block.gpsimd
        def _(pool):
            steps = Steps(pool, pool_step)
            pool.memset(eps[:, :], EPS).then_inc(eps_ready, 1)
            pool.dma_start(pos_i[:, :], positions.rearrange("o (t p) -> p (o t)", p=P),
                           allow_slow_non_contiguous=True).then_inc(pos_loaded, 16)
            pool.dma_start(invf[:, :], inv_freq[0].partition_broadcast(P)).then_inc(pos_loaded, 16)
            steps.link(pool.memset(ident[:, :], 0.0))
            pool.affine_select(out=ident[:, :], in_=ident[:, :], compare_op=ALU.not_equal, fill=1.0, base=0,
                               pattern=[[-1, P]], channel_multiplier=1).then_inc(consts, 1)
            pool.dma_start(stg_b[:, :], conv_ffn[0, 0:2].rearrange("j (c p) -> (j c) p", p=P)).then_inc(conv_loaded, 16)
            ang, a_hi, a_lo, t0, t1 = (trig[:, s, :] for s in (2, 3, 4, 5, 6))
            pool.wait_ge(pos_loaded, 32)
            steps.link(pool.tensor_copy(pos_f[:, :], pos_i[:, :]))
            steps.link(pool.tensor_tensor(ang.rearrange("p (t c) -> p t c", t=NT),
                                   pos_f[:, :].unsqueeze(2).to_broadcast([P, NT, 32]),
                                   invf[:, :].unsqueeze(1).to_broadcast([P, NT, 32]), ALU.mult))
            steps.link(pool.tensor_scalar(t0, ang, 4097.0, None, ALU.mult))
            steps.link(pool.tensor_tensor(t1, t0, ang, ALU.subtract))
            steps.link(pool.tensor_tensor(a_hi, t0, t1, ALU.subtract))
            steps.link(pool.tensor_tensor(a_lo, ang, a_hi, ALU.subtract))
            c1, c2, c3, c4 = split_12bit(1.0 / TWO_PI, 4)
            steps.link(pool.tensor_scalar(acc, a_hi, c4, None, ALU.mult))
            for part, c in ((a_lo, c3), (a_hi, c3), (a_lo, c2)):
                steps.link(pool.tensor_scalar(t0, part, c, None, ALU.mult))
                steps.link(pool.tensor_tensor(acc, acc, t0, ALU.add))
            turns = 0
            for part, c in ((a_lo, c1), (a_hi, c2), (a_hi, c1)):
                steps.link(pool.tensor_scalar(t0, part, c, None, ALU.mult))
                steps.link(pool.tensor_scalar(t1, t0, ROUND, -ROUND, ALU.add, ALU.add))
                steps.link(pool.tensor_tensor(t0, t0, t1, ALU.subtract))
                pool.tensor_tensor(acc, acc, t0, ALU.add).then_inc(turns_ready, 1)
                turns += 1
                pool.wait_ge(turns_ready, turns)
            steps.link(pool.tensor_scalar(t1, acc, ROUND, -ROUND, ALU.add, ALU.add))
            steps.link(pool.tensor_tensor(t0, acc, t1, ALU.subtract))
            pool.tensor_scalar(sin_turns, t0, -0.4999999, 0.4999999, ALU.max, ALU.min).then_inc(angles_ready, 1)
            pool.dma_start(bias_if[0:4, :], i_bias.rearrange("o h -> h o")).then_inc(bias_loaded, 16)
            pool.dma_start(bias_if[32:36, :], f_bias.rearrange("o h -> h o")).then_inc(bias_loaded, 16)
            pool.dma_start(wif_raw[:, :, :], w_in2[:, :, COL_IF:COL_IF + 8]).then_inc(wif_loaded, 16)
            pool.memset(wif_hi[:, :, :].bitcast(F32), 0.0)
            pool.memset(wif_lo[:, :, :].bitcast(F32), 0.0).then_inc(wif_zeroed, 1)
            pool.tensor_tensor(pick[:, :], ident[0:36, 0:MH], ident[0:36, 32:32 + MH], ALU.add)
            pool.memset(neg_m[:, :].bitcast(F32), 0.0).then_inc(neg_m_zeroed, 1)
            pool.memset(mask_ts[:, :], 0.0)
            pool.memset(mask_st[:, :], 0.0)
            pool.wait_ge(consts, 1)
            steps.link(pool.tensor_copy(ident_b[:, :], ident[:, :]))
            steps.link(pool.affine_select(out=mask_ts[:, :], in_=mask_ts[:, :], compare_op=ALU.is_ge, fill=NEG,
                                          base=0, pattern=[[-1, P]], channel_multiplier=1))
            steps.link(pool.affine_select(out=mask_st[:, :], in_=mask_st[:, :], compare_op=ALU.is_ge, fill=NEG,
                                          base=0, pattern=[[1, P]], channel_multiplier=-1))
            pool.memset(ones_r[:, :], 1.0).then_inc(consts, 1)

            pool.wait_ge(conv_done, 8)
            pool.memset(vm[:, :, :, MD:MD + 1], 1.0).then_inc(ones_col, 1)
            wait_full(pool, ("y", 7, 1))
            pool.dma_start(x2[:, :, :], x_v).then_inc(x_again, 16)
            wait_full(pool, ("up", NF - 1, 1))
            pool.dma_start(gF[:, :], norm_final_g.partition_broadcast(P)).then_inc(gf_loaded, 16)

        @block.scalar
        def _(act):
            steps = Steps(act, act_step)
            act.dma_start(stg_a[0:8, :], norm_mix_g[0].rearrange("(k p) -> k p", p=P)).then_inc(params_loaded, 16)
            act.dma_start(stg_a[8:16, :], norm_ffn_g[0].rearrange("(k p) -> k p", p=P)).then_inc(params_loaded, 16)

            def split_hi(n):
                if n == 0:
                    act.wait_ge(raw_loaded[0], 32)
                    for half in (slice(0, 1024), slice(1024, 2048)):
                        act.activation(w_hi[:, 0, half], raw[:, 0, half], ACT.Copy).then_inc(first_hi, 1)
                    return
                act.wait_ge(raw_loaded[n % 2], 32 * (n // 2 + 1))
                wait_slot(act, n)
                act.activation(w_hi[:, n % 4, :], raw[:, n % 2, :], ACT.Copy).then_inc(hi_ready, 1)

            def norm_square(stage, t):
                if stage == 1:
                    act.wait_ge(x_loaded[t], 16)
                    src = x_sb
                else:
                    wait_freed(act, ("out", t, 0))
                    wait_freed(act, ("out", t, 1))
                    src = x2
                if stage == 2 and t >= 2:
                    wait_full(act, (f"norm{stage}", t - 2, 1))
                act.activation(sq1[:, t, :] if stage == 1 else xs[:, t % 2, :], src[:, t, :], ACT.Square,
                               accum_out=ss[:, t:t + 1]).then_inc(sumsq_ready, 1)

            def norm_root(sums, count, at, value, s):
                act.wait_ge(s, value)
                act.activation(root[:, at:at + count], sums, ACT.Sqrt, scale=1.0 / D, bias=eps[:, :]).then_inc(root_ready, 1)

            def norm_xs(first, count):
                act.wait_ge(rstd_ready, first)
                for i in range(count):
                    t = first + i
                    if t >= 2:
                        wait_full(act, ("norm1", t - 2, 1))
                    act.activation(xs[:, t % 2, :], x_sb[:, t, :], ACT.Copy, scale=rstd[:, i:i + 1]).then_inc(xs_ready, 1)

            act.wait_ge(eps_ready, 1)
            act.activation(root[:, 15:16], eps[:, :], ACT.Sqrt)

            def norm_hi(stage, t):
                for j in range(2):
                    wait_freed(act, (f"norm{stage}", t, j))
                    act.activation(hT_hi[:, 4 * j:4 * j + 4, t * P:(t + 1) * P], h32[:, t % 2, j, :, :],
                                   ACT.Copy).then_inc(h_hi_ready, 1)

            norm_square(1, 0)
            norm_root(ss[:, 0:1], 1, 0, 1, sumsq_ready)
            split_hi(0)
            norm_hi(1, 0)
            norm_square(1, 1)
            norm_root(ss[:, 1:2], 1, 1, 2, sumsq_ready)
            split_hi(1)
            norm_square(1, 2)
            norm_xs(1, 1)
            norm_square(1, 3)
            norm_root(ss[:, 2:4], 2, 2, 4, sumsq_ready)
            norm_hi(1, 1)
            act.activation(root[:, 15:16], eps[:, :], ACT.Sin)
            norm_xs(2, 2)
            norm_hi(1, 2)

            def attn_exp(g):
                i, hp = g // 4, g % 4
                n = (i + 1) * P
                act.wait_ge(max_ready, g + 1)
                for e in range(2):
                    if g >= 1:
                        wait_full(act, ("probT", g - 1, e))
                    if hp == 0 and e == 0 and i >= 2:
                        wait_freed(act, ("attn", i - 2))
                    h = 2 * hp + e
                    act.activation(prob[:, e, 0:n], B(("score", g, e))[:, 0:n], ACT.Exp, bias=nmax[:, g % 2, e:e + 1],
                                   accum_out=rsum[:, i % 2, h:h + 1]).then_inc(freesem(("score", g, e)), 1)

            def attn_probT(g):
                n = (g // 4 + 1) * P
                wait_full(act, ("probT", g, 0))
                if g >= 1:
                    act.wait_ge(pv_done, 2 * g - 1)
                act.copy(probT[:, 0, 0:n], B(("probT", g, 0))[:, 0:n]).then_inc(freesem(("probT", g, 0)), 1)

            def mlstm_exp(g):
                i, hp = g // 2, g % 2
                if i == 0:
                    wait_freed(act, ("decay", 0))
                else:
                    act.wait_ge(em_ready, i)
                if g >= 1:
                    wait_full(act, ("mnum", g - 1))
                else:
                    wait_full(act, ("probT", 15, 1))
                for e in range(2):
                    h = 2 * hp + e
                    for j in range(i + 1):
                        col = 4 * (i * (i + 1) // 2 + j) + h
                        src = em[:, 0, h * P:(h + 1) * P] if j == i else B(("decay", i))[:, h * P:(h + 1) * P]
                        ins = act.activation(prob[:, e, j * P:(j + 1) * P], src, ACT.Exp, bias=gcol[:, col:col + 1])
                        if hp == 1 and e == 1 and i >= 1 and j == i - 1:
                            ins.then_inc(freesem(("decay", i)), 1)
                    ins.then_inc(decay_ready, 1)

            for c in range(NBLK):
                tag = ("block", c)
                if c % 2 == 0 and c:
                    split_hi(c // 2 + 2)
                if c == 0:
                    act.wait_ge(angles_ready, 2)
                    act.activation(cosT[:, :, :], cos_turns.rearrange("p (t c) -> p t c", t=NT), ACT.Sin, scale=TWO_PI)
                    act.activation(sinT[:, :, 0, :], sin_turns.rearrange("p (t c) -> p t c", t=NT), ACT.Sin,
                                   scale=-TWO_PI)
                    act.activation(sinT[:, :, 1, :], sin_turns.rearrange("p (t c) -> p t c", t=NT), ACT.Sin,
                                   scale=TWO_PI).then_inc(trig_ready, 1)
                if c == 1:
                    norm_hi(1, 3)
                    split_hi(2)
                if c == 2:
                    act.wait_ge(wif_loaded, 16)
                    act.wait_ge(wif_zeroed, 1)
                    act.activation(wif_hi[:, :, 0:4], wif_raw[:, :, 0:4], ACT.Copy)
                    act.activation(wif_hi[:, :, 32:36], wif_raw[:, :, 4:8], ACT.Copy).then_inc(wif_hi_ready, 1)
                if c == 6:
                    act.wait_ge(bias_loaded, 32)
                    wait_full(act, ("gates_if",))
                    act.activation(rows[:, 0, :], ps[32:36, 4, :], ACT.Identity, bias=bias_if[32:36, :]).then_inc(f_row, 1)
                    act.activation(rows[:, 3, :], ps[0:4, 4, :], ACT.Identity, bias=bias_if[0:4, :]).then_inc(bank_free[4], 1)
                if c == 8:
                    act.wait_ge(f_abs, 1)
                    steps.link(act.activation(rows[:, 1, :], rows[:, 1, :], ACT.Exp, scale=-1.0))
                    act.activation(rows[:, 1, :], rows[:, 1, :], ACT.Ln, bias=1.0).then_inc(f_ln, 1)
                if 12 <= c < 20:
                    m = c - 12
                    wait_full(act, tag)
                    if m >= 2:
                        act.wait_ge(conv_done, m - 1)
                    act.activation(cacc[:, m % 2, :], B(tag), ACT.Copy, scale=tap_m(3, m)).then_inc(conv_tap, 1)
                elif 8 <= c < 12:
                    wait_full(act, tag)
                    act.copy(va[:, c - 8, :], B(tag)).then_inc(freesem(tag), 1)
                elif 20 <= c < 24:
                    wait_full(act, tag)
                    if c == 20:
                        act.wait_ge(conv_done, 8)
                    act.activation(vm[:, c - 20, :, 0:MD], B(tag).rearrange("p (h d) -> p h d", h=MH),
                                   ACT.Copy).then_inc(freesem(tag), 1)
                elif 24 <= c < 28:
                    wait_full(act, tag)
                    act.activation(o_sig[:, c - 24, :], B(tag), ACT.Tanh, scale=0.5).then_inc(freesem(tag), 1)
                    wait_freed(act, tag)
                    act.activation(o_sig[:, c - 24, :], o_sig[:, c - 24, :], ACT.Copy, scale=0.5,
                                   bias=0.5).then_inc(o_ready, 1)
                elif c >= 28:
                    wait_full(act, tag)
                    dst = (gate_a0, gate_m, gate_a1)[(c - 28) // 4]
                    act.activation(dst[:, c % 4, :], B(tag), ACT.Tanh, scale=0.5).then_inc(freesem(tag), 1)
                if 2 <= c <= 9:
                    r = c - 2
                    rt = ("rope", r)
                    wait_full(act, rt)
                    dst = (qT_hi if r < NT else kT_hi)[:, :, (r % NT) * P:(r % NT + 1) * P]
                    act.activation(dst, B(rt).rearrange("p (h t) -> p h t", h=4), ACT.Copy,
                                   scale=0.125 if r < NT else 1.0).then_inc(qk_hi_ready, 1)
                if c == 12:
                    wait_freed(act, ("cols_if",))
                    act.activation(expm[:, :], gcol[:, 40:56], ACT.Exp).then_inc(expm_ready, 1)
                if 0 <= c - ATT < 16:
                    attn_exp(c - ATT)
                if 0 <= c - ATT - 1 < 16:
                    attn_probT(c - ATT - 1)
                if 0 <= c - ATT - 6 <= 12 and (c - ATT - 6) % 4 == 0:
                    i = (c - ATT - 6) // 4
                    wait_full(act, ("attnT", i))
                    act.activation(atT_hi[:, :, i * P:(i + 1) * P],
                                   B(("attnT", i)).rearrange("p (k t) -> p k t", k=4), ACT.Copy).then_inc(at_hi_ready, 1)
                if 12 <= c < 20:
                    m = c - 12
                    wait_freed(act, tag)
                    act.activation(cth[:, m % 2, :], cacc[:, m % 2, :], ACT.Tanh, scale=0.5).then_inc(conv_tanh, 1)
                if 0 <= c - MLS < 8:
                    mlstm_exp(c - MLS)
                if 0 <= c - MLS - 4 <= 6 and (c - MLS - 4) % 2 == 0:
                    i = (c - MLS - 4) // 2
                    wait_freed(act, ("mT", i))
                    act.activation(hmT_hi[:, :, i * P:(i + 1) * P], h_tok(i).rearrange("p (k t) -> p k t", k=4),
                                   ACT.Copy).then_inc(hm_hi_ready, 1)
                if 0 <= c - MLS - 1 < 8:
                    g = c - MLS - 1
                    act.wait_ge(hm_raw, g + 1)
                    if g >= 1:
                        act.wait_ge(hm_sq, g)
                    for e in range(2):
                        h = 2 * (g % 2) + e
                        ins = act.activation(junk[:, e, :], h_tok(g // 2)[:, h * P:(h + 1) * P], ACT.Square,
                                             accum_out=ss[:, 4 + h:5 + h])
                    ins.then_inc(hm_sq, 1)

            def merge_hi(n):
                act.wait_ge(m32_ready, n + 1)
                dst = (mrg_hi0, mrg_hi1)[n // 4]
                act.activation(dst[:, n % 4, :], prob[:, n % 2, :], ACT.Copy, scale=0.5).then_inc(mrg_hi_ready, 1)

            for n in range(4):
                if n in (0, 1):
                    split_hi(2 * U_GM1 + n)
                merge_hi(n)
            split_hi(2 * U_B0 + 4)
            split_hi(2 * U_B0 + 5)
            for m in range(4):
                wait_full(act, ("gate", m))
                if m == 0:
                    act.wait_ge(m32_ready, 4)
                act.activation(gate_m[:, m, :], B(("gate", m)), ACT.Tanh, scale=0.5).then_inc(freesem(("gate", m)), 1)
            split_hi(2 * U_GM1 + 4)
            split_hi(2 * U_GM1 + 5)
            for n in range(4, 7):
                merge_hi(n)
            split_hi(2 * U_B1 + 4)
            merge_hi(7)
            split_hi(2 * U_B1 + 5)
            for t in range(NT - 1):
                norm_square(2, t)
                norm_root(ss[:, t:t + 1], 1, 4 + t, 5 + t, sumsq_ready)
                norm_hi(2, t)
            split_hi(2 * U_O0 + 4)
            norm_square(2, 3)
            norm_root(ss[:, 3:4], 1, 7, 8, sumsq_ready)
            split_hi(2 * U_O0 + 5)
            norm_hi(2, 3)
            split_hi(2 * U_O1 + 4)
            split_hi(2 * U_O1 + 5)

            def glu(g, f, n, it):
                f0 = g * GROUP[0]
                for s in range(2):
                    bank, _, full = plan[("up", f, s)]
                    act.wait_ge(bank_full[bank], 2 * it + full)
                    act.activation(cv[:, f % 2, s, :], ps[:, bank, :], ACT.Copy,
                                   scale=tap_f(2, 4 * it + (f + NF * s))).then_inc(glu_tap, 1)
                m = n + 4
                act.wait_ge(raw_loaded[m % 2], 32 * (m // 2 + 1) + 64 * it)
                act.activation(w_hi[:, m % 4, :], raw[:, m % 2, :], ACT.Copy).then_inc(hi_ready, 1)
                bank, k, _ = plan[("up", f, 0)]
                act.wait_ge(bank_free[bank], 2 * it + (k + 1))
                if f >= 2:
                    act.wait_ge(act_ready, 4 * it + (f - 1))
                act.activation(sil[:, f % 2, :], cv[:, f % 2, 0, :], ACT.Silu).then_inc(glu_silu, 1)
                act.wait_ge(glu_prod, 4 * it + (f + 1))
                act.activation(act_hi[:, bass.ds(4 * it + (f - f0), 1), :], sil[:, f % 2:f % 2 + 1, :],
                               ACT.Copy).then_inc(glu_hi, 1)

            for g in range(2):
                f0, n0 = g * GROUP[0], N_UP[g]
                first = 0
                if g == 0:
                    for j in range(4):
                        glu(g, f0 + j, n0 + j, 0)
                    first = 4
                loops = (GROUP[g] - first) // 4
                with act.Fori(0, loops) as it:
                    for j in range(4):
                        glu(g, f0 + first + j, n0 + first + j, it)
                for j in range(first + 4 * loops, GROUP[g]):
                    glu(g, f0 + j, n0 + j, 0)
                for d in range(GROUP[g] // 2):
                    if N_DOWN[g] + d + 4 < N_LOADS:
                        split_hi(N_DOWN[g] + d + 4)
            act.activation(root[:, 15:16], eps[:, :], ACT.Sqrt)
            for t in range(NT):
                for n in range(2):
                    wait_freed(act, ("down", 1, t, n))
                    act.activation(cv[:, n, t % 2, :], x2[:, t, n * 512:(n + 1) * 512], ACT.Square,
                                   accum_out=ss[:, 2 * t + n:2 * t + n + 1]).then_inc(final_sq, 1)
                norm_root(ss[:, 8 + t:9 + t], 1, 8 + t, t + 1, final_sum)
            act.wait_ge(last_rstd, 1)
            act.wait_ge(last_gain, 1)
            act.activation(out_sb[:, NT - 1, 512:], sil[:, 0, :], ACT.Copy, scale=rstd[:, 0:1]).then_inc(out_ready, 1)

        @block.vector
        def _(dve):
            steps = Steps(dve, dve_step)
            link, mark = steps.link, steps.mark

            def split_lo(n):
                dve.wait_ge(hi_ready, n)
                dve.tensor_tensor(w_lo[:, n % 4, :], raw[:, n % 2, :], w_hi[:, n % 4, :].bitcast(F32),
                                  ALU.subtract).then_inc(lo_ready, 1)

            def rsqrt(sums, count, cols):
                v, y, t = var[:, 0:cols], rstd[:, 0:cols], newt[:, 0:cols]
                link(dve.tensor_scalar(v, sums, 1.0 / count, EPS, ALU.mult, ALU.add))
                link(dve.tensor_scalar(seed_i[:, 0:cols], v.bitcast(I32), 1, None, ALU.logical_shift_right))
                link(dve.tensor_scalar(y.bitcast(I32), seed_i[:, 0:cols], -1.0, float(0x5F3759DF), ALU.mult, ALU.add))
                for _ in range(3):
                    link(dve.scalar_tensor_tensor(t, y, -0.5, y, ALU.mult, ALU.mult))
                    link(dve.tensor_tensor(t, t, v, ALU.mult))
                    link(dve.scalar_tensor_tensor(y, t, 1.5, y, ALU.add, ALU.mult))

            def rsqrt_from_root(sums, root, cols, roots):
                v, y, t = var[:, 0:cols], rstd[:, 0:cols], newt[:, 0:cols]
                link(dve.tensor_scalar(v, sums, 1.0 / D, EPS, ALU.mult, ALU.add))
                dve.wait_ge(root_ready, roots)
                link(dve.reciprocal(y, root))
                link(dve.scalar_tensor_tensor(t, y, -0.5, y, ALU.mult, ALU.mult))
                link(dve.tensor_tensor(t, t, v, ALU.mult))
                link(dve.scalar_tensor_tensor(y, t, 1.5, y, ALU.add, ALU.mult))

            def norm_scale(stage, first, count):
                src = x_sb if stage == 1 else x2
                dve.wait_ge(sumsq_ready, 4 * (stage - 1) + first + count)
                at = 4 * (stage - 1) + first
                if at in (2, 4):
                    dve.wait_ge(xs_ready, at)
                rsqrt_from_root(ss[:, first:first + count], root[:, at:at + count], count, at + 1 if stage == 1 else at)
                if stage == 1 and first:
                    dve.nop().then_inc(rstd_ready, 1)
                    return
                for i in range(count):
                    t = first + i
                    dve.tensor_scalar(xs[:, t % 2, :], src[:, t, :], rstd[:, i:i + 1], None,
                                      ALU.mult).then_inc(xs_ready, 1)

            def norm_gain(stage, t):
                gT = g1T if stage == 1 else g2T
                for j in range(2):
                    tag = (f"norm{stage}", t, j)
                    wait_full(dve, tag)
                    if stage == 1 and t == 0 and j == 0:
                        dve.wait_ge(params_ready, 1)
                    dve.tensor_tensor(h32[:, t % 2, j, :, :], B(tag).rearrange("p (k t) -> p k t", k=4),
                                      gT[:, 4 * j:4 * j + 4].unsqueeze(2).to_broadcast([P, 4, P]),
                                      ALU.mult).then_inc(freesem(tag), 1)

            def norm_lo(stage, t, only=None):
                for j in range(2) if only is None else (only,):
                    dve.wait_ge(h_hi_ready, 8 * (stage - 1) + 2 * t + j + 1)
                    sl = slice(t * P, (t + 1) * P)
                    dve.tensor_tensor(hT_lo[:, 4 * j:4 * j + 4, sl], h32[:, t % 2, j, :, :],
                                      hT_hi[:, 4 * j:4 * j + 4, sl].bitcast(F32), ALU.subtract).then_inc(hT_ready, 1)

            norm_scale(1, 0, 1)
            dve.wait_ge(stage_T, 1)
            dve.tensor_copy(par_a[:, :], ps[:, 6, 0:96]).then_inc(params_ready, 1)
            norm_gain(1, 0)
            for half, cols in enumerate((slice(0, 1024), slice(1024, 2048))):
                dve.wait_ge(first_hi, half + 1)
                dve.tensor_tensor(w_lo[:, 0, cols], raw[:, 0, cols], w_hi[:, 0, cols].bitcast(F32),
                                  ALU.subtract).then_inc(lo_ready if half else first_lo, 1)
                norm_lo(1, 0, half)
            norm_scale(1, 1, 1)
            split_lo(1)
            norm_gain(1, 1)
            norm_lo(1, 1)
            norm_scale(1, 2, 2)
            t0, t1 = trig[:, 2, :], trig[:, 3, :]
            dve.wait_ge(turns_ready, 3)
            link(dve.tensor_scalar(t0, acc, 0.25, None, ALU.add))
            link(dve.tensor_scalar(t1, t0, ROUND, -ROUND, ALU.add, ALU.add))
            link(dve.tensor_tensor(t0, t0, t1, ALU.subtract))
            dve.tensor_scalar(cos_turns, t0, -0.4999999, 0.4999999, ALU.max, ALU.min).then_inc(angles_ready, 1)
            norm_gain(1, 2)
            norm_lo(1, 2)
            dve.wait_ge(stage_T, 2)
            dve.tensor_copy(par_b[:, :], ps[:, 7, 0:88]).then_inc(params_ready, 1)

            def rope(c):
                t, tag, b = c % NT, ("block", c), c % 2
                wait_full(dve, tag)
                src = B(tag).rearrange("p (h s c) -> p h s c", h=AH, s=2)
                m1 = rp[:, b, 0, :].rearrange("p (h s c) -> p h s c", h=AH, s=2)
                m2 = rp[:, b, 1, :].rearrange("p (h s c) -> p h s c", h=AH, s=2)
                cb = cosT[:, t, :].unsqueeze(1).to_broadcast([P, 2 * AH, 32])
                dve.tensor_tensor(rp[:, b, 0, :].rearrange("p (h c) -> p h c", c=32),
                                  B(tag).rearrange("p (h c) -> p h c", c=32), cb, ALU.mult)
                for s in range(2):
                    sb = sinT[:, t, s, :].unsqueeze(1).to_broadcast([P, AH, 32])
                    ins = dve.tensor_tensor(m2[:, :, s, :], src[:, :, 1 - s, :], sb, ALU.mult)
                ins.then_inc(freesem(tag), 1)
                wait_freed(dve, tag)
                if c >= 2:
                    wait_full(dve, ("rope", c - 2))
                dve.tensor_tensor(qr[:, b, :], rp[:, b, 0, :], rp[:, b, 1, :], ALU.add).then_inc(rope_done, 1)

            def if_rows():
                r = lambda k: rows[:, k, :]
                seg = lambda k, t: rows[:, k, t * P:(t + 1) * P]
                dve.wait_ge(consts, 2)
                dve.wait_ge(f_row, 1)
                dve.scalar_tensor_tensor(r(1), r(0), -1.0, r(0), ALU.mult, ALU.max).then_inc(f_abs, 1)
                dve.wait_ge(f_ln, 1)
                link(dve.scalar_tensor_tensor(r(0), r(0), 0.0, r(1), ALU.min, ALU.subtract))
                for t in range(NT):
                    n = mark(dve.tensor_tensor_scan(seg(2, t), ones_r[:, :], seg(0, t), 0.0, ALU.mult, ALU.add))
                dve.wait_ge(dve_step, n)
                wait_freed(dve, ("gates_if",))
                for t in range(NT):
                    n = mark(dve.tensor_tensor(seg(4 + t, t), seg(3, t), seg(2, t), ALU.subtract))
                dve.wait_ge(dve_step, n)
                for t in range(NT):
                    total = rows[:, 2, t * P - 1:t * P] if t else None
                    if t:
                        link(dve.tensor_tensor(carry[:, t:t + 1], rows[:, 1, t * P - 1:t * P], total, ALU.add))
                        mark(dve.tensor_scalar(rows[:, 4 + t, 0:t * P], rows[:, 3 + t, 0:t * P], total, None, ALU.add))
                    link(dve.tensor_tensor_scan(seg(1, t), ones_r[:, :], seg(4 + t, t),
                                                carry[:, t:t + 1] if t else 0.0, ALU.mult, ALU.max))
                dve.wait_ge(neg_m_zeroed, 1)
                link(dve.tensor_scalar(neg_m[0:4, :], r(1), -1.0, None, ALU.mult))
                dve.scalar_tensor_tensor(neg_m[32:36, :], r(1), -1.0, neg_m[0:4, :].bitcast(F32), ALU.mult, ALU.subtract)
                dve.scalar_tensor_tensor(r(0), r(1), -1.0, r(2), ALU.mult, ALU.subtract).then_inc(rows_ready, 1)

            def attn_max(g):
                n = (g // 4 + 1) * P
                wait_full(dve, ("score", g, 0))
                wait_full(dve, ("score", g, 1))
                dve.reduce_max(nmax[:, g % 2, :], ps[:, 2:4, 0:n], axis=AX_X, negate=True).then_inc(max_ready, 1)

            def attn_probT(g):
                n = (g // 4 + 1) * P
                wait_full(dve, ("probT", g, 1))
                if g >= 1:
                    dve.wait_ge(pv_done, 2 * g)
                dve.tensor_copy(probT[:, 1, 0:n], B(("probT", g, 1))[:, 0:n]).then_inc(freesem(("probT", g, 1)), 1)

            def attn_out(i):
                dve.wait_ge(pv_done, 8 * i + 8)
                wait_freed(dve, ("score", 4 * i + 3, 1))
                link(dve.reciprocal(rinv[:, :], rsum[:, i % 2, :]))
                tag = ("attn", i)
                if i >= 2:
                    wait_full(dve, ("attnT", i - 2))
                dve.tensor_tensor(tok_a[:, i % 2, :].rearrange("p (h d) -> p h d", h=AH),
                                  B(tag).rearrange("p (h d) -> p h d", h=AH),
                                  rinv[:, :].unsqueeze(2).to_broadcast([P, AH, AD]), ALU.mult).then_inc(freesem(tag), 1)

            def decay_mask(i):
                tag = ("decay", i)
                wait_full(dve, tag)
                if i:
                    dve.wait_ge(decay_ready, 4 * i)
                else:
                    dve.wait_ge(pv_done, 32)
                ins = dve.tensor_tensor(em[:, 0, :].rearrange("p (h t) -> p h t", h=MH),
                                        B(tag).rearrange("p (h t) -> p h t", h=MH),
                                        mask_st[:, :].unsqueeze(1).to_broadcast([P, MH, P]), ALU.add)
                ins.then_inc(em_ready if i else freesem(tag), 1)

            def mlstm_scores(g):
                i = g // 2
                n = (i + 1) * P
                for e in range(2):
                    tag = ("mscore", g, e)
                    wait_full(dve, tag)
                    dve.wait_ge(decay_ready, 2 * g + e + 1)
                    dve.scalar_tensor_tensor(prob[:, e, 0:n], B(tag)[:, 0:n], 0.25 * MD ** -0.5, prob[:, e, 0:n],
                                             ALU.mult, ALU.mult).then_inc(freesem(tag), 1)

            def mlstm_out(g):
                i, hp, tag = g // 2, g % 2, ("mnum", g)
                wait_full(dve, tag)
                num = B(tag)[:, 0:2 * (MD + 1)].rearrange("p (e d) -> p e d", e=2)
                if g == 0:
                    dve.wait_ge(expm_ready, 1)
                link(dve.tensor_scalar(dinv[:, :].unsqueeze(2), num[:, :, MD:MD + 1], -1.0, None, ALU.mult))
                link(dve.tensor_tensor(den[:, :].unsqueeze(2), num[:, :, MD:MD + 1], dinv[:, :].unsqueeze(2), ALU.max))
                link(dve.tensor_tensor(den[:, :], den[:, :], expm[:, 4 * i + 2 * hp:4 * i + 2 * hp + 2], ALU.max))
                link(dve.reciprocal(dinv[:, :], den[:, :]))
                if hp == 0 and i >= 2:
                    dve.wait_ge(hm_hi_ready, i - 1)
                mark(dve.tensor_tensor(h_tok(i)[:, 256 * hp:256 * hp + 256].rearrange("p (e d) -> p e d", e=2),
                                       num[:, :, 0:MD], dinv[:, :].unsqueeze(2).to_broadcast([P, 2, MD]), ALU.mult))
                dve.wait_ge(dve_step, steps.n)
                dve.nop().then_inc(freesem(tag), 1)
                dve.nop().then_inc(hm_raw, 1)

            def mlstm_norm(i):
                dve.wait_ge(hm_sq, 2 * i + 2)
                rsqrt(ss[:, 4:8], MD, 4)
                dve.wait_ge(o_ready, i + 1)
                for h in range(MH):
                    sl = slice(h * P, (h + 1) * P)
                    ins = dve.scalar_tensor_tensor(h_tok(i)[:, sl], h_tok(i)[:, sl], rstd[:, h:h + 1], o_sig[:, i, sl],
                                                   ALU.mult, ALU.mult)
                ins.then_inc(hm_ready, 1)

            def mlstm_gain(i):
                tag = ("mT", i)
                wait_full(dve, tag)
                dve.tensor_tensor(h_tok(i).rearrange("p (k t) -> p k t", k=4),
                                  B(tag).rearrange("p (k t) -> p k t", k=4),
                                  mgT.unsqueeze(2).to_broadcast([P, 4, P]), ALU.mult).then_inc(freesem(tag), 1)
                dve.wait_ge(hm_hi_ready, i + 1)
                sl = slice(i * P, (i + 1) * P)
                dve.tensor_tensor(hmT_lo[:, :, sl], h_tok(i).rearrange("p (k t) -> p k t", k=4),
                                  hmT_hi[:, :, sl].bitcast(F32), ALU.subtract).then_inc(hmT_ready, 1)

            def rope_lo(r):
                rt = ("rope", r)
                dve.wait_ge(qk_hi_ready, r + 1)
                hi, lo = (qT_hi, qT_lo) if r < NT else (kT_hi, kT_lo)
                sl = slice((r % NT) * P, (r % NT + 1) * P)
                dve.scalar_tensor_tensor(lo[:, :, sl], B(rt).rearrange("p (h t) -> p h t", h=4),
                                         0.125 if r < NT else 1.0, hi[:, :, sl].bitcast(F32), ALU.mult,
                                         ALU.subtract).then_inc(freesem(rt), 1)

            for c in range(NBLK):
                tag = ("block", c)
                if 13 <= c <= 20:
                    m = c - 13
                    dve.wait_ge(conv_tanh, m + 1)
                    dst = (qmT if m < 4 else kmT)[:, m % 4, :]
                    dve.scalar_tensor_tensor(dst, cth[:, m % 2, :], 1.0, cacc[:, m % 2, :], ALU.add,
                                             ALU.mult).then_inc(conv_done, 1)
                if 0 <= c - ATT - 5 <= 12 and (c - ATT - 5) % 4 == 0:
                    attn_out((c - ATT - 5) // 4)
                if c == 0:
                    dve.wait_ge(trig_ready, 1)
                if c == 1:
                    norm_gain(1, 3)
                    norm_lo(1, 3)
                if 3 <= c <= 10:
                    rope_lo(c - 3)
                if c < 8:
                    rope(c)
                if c == 8:
                    if_rows()
                if c == 3:
                    dve.wait_ge(wif_hi_ready, 1)
                    dve.tensor_tensor(wif_lo[:, :, 0:4], wif_raw[:, :, 0:4], wif_hi[:, :, 0:4].bitcast(F32), ALU.subtract)
                    dve.tensor_tensor(wif_lo[:, :, 32:36], wif_raw[:, :, 4:8], wif_hi[:, :, 32:36].bitcast(F32),
                                      ALU.subtract).then_inc(wif_ready, 1)
                if 12 <= c < 20:
                    m = c - 12
                    a = cacc[:, m % 2, :]
                    dve.wait_ge(conv_tap, m + 1)
                    for sh in (1, 2, 3):
                        ins = dve.scalar_tensor_tensor(a[:, sh:], B(tag)[:, 0:SEQ - sh], tap_m(3 - sh, m), a[:, sh:],
                                                       ALU.mult, ALU.add)
                        if sh < 3:
                            link(ins)
                        else:
                            ins.then_inc(freesem(tag), 1)
                if c == 11:
                    wait_full(dve, ("cols_if",))
                    dve.tensor_copy(gcol[:, :], B(("cols_if",))[:, 0:56]).then_inc(freesem(("cols_if",)), 1)
                if 0 <= c - ATT < 16:
                    attn_max(c - ATT)
                if 0 <= c - ATT - 1 < 16:
                    attn_probT(c - ATT - 1)
                if 0 <= c - ATT - 6 <= 12 and (c - ATT - 6) % 4 == 0:
                    i = (c - ATT - 6) // 4
                    dve.wait_ge(at_hi_ready, i + 1)
                    sl = slice(i * P, (i + 1) * P)
                    dve.tensor_tensor(atT_lo[:, :, sl], B(("attnT", i)).rearrange("p (k t) -> p k t", k=4),
                                      atT_hi[:, :, sl].bitcast(F32), ALU.subtract).then_inc(freesem(("attnT", i)), 1)
                if 0 <= c - MLS < 8:
                    if (c - MLS) % 2 == 0:
                        decay_mask((c - MLS) // 2)
                    mlstm_scores(c - MLS)
                if 0 <= c - MLS - 4 <= 6 and (c - MLS - 4) % 2 == 0:
                    mlstm_gain((c - MLS - 4) // 2)
                if 0 <= c - MLS - 1 < 8:
                    mlstm_out(c - MLS - 1)
                    if (c - MLS - 1) % 2 == 1:
                        mlstm_norm((c - MLS - 1) // 2)
                if c % 2 == 0 and c or c == 1:
                    split_lo(c // 2 + 2)

            def gated(n, s):
                if n == 0:
                    wait_freed(dve, ("block", 39))
                if n == 4:
                    wait_freed(dve, ("gate", 3))
                gate = ((gate_a0, gate_a1)[n // 4], gate_m)[s][:, n % 4, :]
                tag = ("y", n, s)
                wait_full(dve, tag)
                dve.scalar_tensor_tensor((prob, probT)[s][:, n % 2, :], gate, 1.0, B(tag), ALU.add,
                                         ALU.mult).then_inc(freesem(tag), 1)

            def merge(n):
                if n < 7:
                    gated(n, 0)
                gated(n, 1)
                wait_freed(dve, ("y", n, 0))
                wait_freed(dve, ("y", n, 1))
                dve.tensor_tensor(prob[:, n % 2, :], prob[:, n % 2, :], probT[:, n % 2, :], ALU.add).then_inc(m32_ready, 1)
                dve.wait_ge(mrg_hi_ready, n + 1)
                hi, lo = ((mrg_hi0, mrg_lo0), (mrg_hi1, mrg_lo1))[n // 4]
                dve.scalar_tensor_tensor(lo[:, n % 4, :], prob[:, n % 2, :], 0.5, hi[:, n % 4, :].bitcast(F32),
                                         ALU.mult, ALU.subtract).then_inc(mrg_ready, 1)

            for n in range(4):
                merge(n)
                if n in (0, 1):
                    split_lo(2 * U_GM1 + n)
            split_lo(2 * U_B0 + 4)
            split_lo(2 * U_B0 + 5)
            split_lo(2 * U_GM1 + 4)
            split_lo(2 * U_GM1 + 5)
            for n in range(4, 7):
                merge(n)
            gated(7, 0)
            split_lo(2 * U_B1 + 4)
            merge(7)
            split_lo(2 * U_B1 + 5)

            def residual(t, n):
                if t == 0 and n == 0:
                    dve.wait_ge(x_again, 16)
                tag = ("out", t, n)
                wait_full(dve, tag)
                sl = x2[:, t, n * 512:(n + 1) * 512]
                dve.tensor_tensor(sl, B(tag), sl, ALU.add).then_inc(freesem(tag), 1)

            for t in range(NT - 1):
                residual(t, 0)
                residual(t, 1)
                norm_scale(2, t, 1)
                norm_gain(2, t)
                norm_lo(2, t)
            residual(3, 0)
            split_lo(2 * U_O0 + 4)
            residual(3, 1)
            norm_scale(2, 3, 1)
            split_lo(2 * U_O0 + 5)
            norm_gain(2, 3)
            norm_lo(2, 3)
            split_lo(2 * U_O1 + 4)
            split_lo(2 * U_O1 + 5)

            def glu(g, f, n, it, step):
                f0 = g * GROUP[0]
                banks = [plan[("up", f, s)] for s in range(2)]
                for sh in (1, 2):
                    for s in range(2):
                        a = cv[:, f % 2, s, :]
                        if sh == 1:
                            dve.wait_ge(glu_tap, 8 * it + (2 * f + s + 1))
                        else:
                            dve.wait_ge(dve_step, step + (s + 1))
                        ins = dve.scalar_tensor_tensor(a[:, sh:], ps[:, banks[s][0], 0:SEQ - sh],
                                                       tap_f(2 - sh, 4 * it + (f + NF * s)), a[:, sh:],
                                                       ALU.mult, ALU.add)
                        ins.then_inc(dve_step if sh == 1 else bank_free[banks[s][0]], 1)
                m = n + 4
                dve.wait_ge(hi_ready, 4 * it + m)
                dve.tensor_tensor(w_lo[:, m % 4, :], raw[:, m % 2, :], w_hi[:, m % 4, :].bitcast(F32),
                                  ALU.subtract).then_inc(lo_ready, 1)
                dve.wait_ge(glu_silu, 4 * it + (f + 1))
                dve.wait_ge(bank_free[banks[1][0]], 2 * it + (banks[1][1] + 1))
                dve.tensor_tensor(sil[:, f % 2, :], sil[:, f % 2, :], cv[:, f % 2, 1, :], ALU.mult).then_inc(glu_prod, 1)
                dve.wait_ge(glu_hi, 4 * it + (f + 1))
                sl = bass.ds(4 * it + (f - f0), 1)
                dve.tensor_tensor(act_lo[:, sl, :], sil[:, f % 2:f % 2 + 1, :], act_hi[:, sl, :].bitcast(F32),
                                  ALU.subtract).then_inc(act_ready, 1)

            for g in range(2):
                f0, n0 = g * GROUP[0], N_UP[g]
                first = 0
                if g == 0:
                    for j in range(4):
                        glu(g, f0 + j, n0 + j, 0, steps.n)
                        steps.n += 2
                    first = 4
                loops = (GROUP[g] - first) // 4
                with dve.Fori(0, loops) as it:
                    for j in range(4):
                        glu(g, f0 + first + j, n0 + first + j, it, 8 * it + (steps.n + 2 * j))
                steps.n += 8 * loops
                for j in range(first + 4 * loops, GROUP[g]):
                    glu(g, f0 + j, n0 + j, 0, steps.n)
                    steps.n += 2
                for d in range(GROUP[g] // 2 - 1):
                    if N_DOWN[g] + d + 4 < N_LOADS:
                        split_lo(N_DOWN[g] + d + 4)
                for t in range(NT):
                    for n in range(2):
                        tag = ("down", g, t, n)
                        wait_full(dve, tag)
                        sl = x2[:, t, n * 512:(n + 1) * 512]
                        if g == 1:
                            wait_freed(dve, ("down", 0, t, n))
                        else:
                            wait_freed(dve, ("out", t, n))
                        dve.tensor_tensor(sl, B(tag), sl, ALU.add).then_inc(freesem(tag), 1)
                    if g == 1:
                        if t == 0:
                            dve.wait_ge(gf_loaded, 16)
                        if t == NT - 1:
                            wait_freed(dve, ("down", 1, t, 1))
                            dve.tensor_tensor(sil[:, 0, :], x2[:, t, 512:], gF[:, 512:], ALU.mult).then_inc(last_gain, 1)
                        dve.wait_ge(final_sq, 2 * t + 2)
                        dve.tensor_tensor(ss[:, 8 + t:9 + t], ss[:, 2 * t:2 * t + 1], ss[:, 2 * t + 1:2 * t + 2],
                                          ALU.add).then_inc(final_sum, 1)
                        dve.wait_ge(final_sum, t + 1)
                        rsqrt_from_root(ss[:, 8 + t:9 + t], root[:, 8 + t:9 + t], 1, 8 + t)
                        if t == NT - 1:
                            dve.nop().then_inc(last_rstd, 1)
                        half = slice(0, 512) if t == NT - 1 else slice(0, D)
                        dve.scalar_tensor_tensor(out_sb[:, t, half], x2[:, t, half], rstd[:, 0:1], gF[:, half], ALU.mult,
                                                 ALU.mult).then_inc(last_ready if t == NT - 1 else out_ready, 1)
                if g == 0:
                    split_lo(N_DOWN[0] + GROUP[0] // 2 + 3)

        @block.tensor
        def _(pe):
            def mm3(dst, l_hi, l_lo, r_hi, r_lo, start, stop):
                pe.matmul(dst, l_hi, r_hi, start=start, stop=False)
                pe.matmul(dst, l_hi, r_lo, start=False, stop=False)
                return pe.matmul(dst, l_lo, r_hi, start=False, stop=stop)

            def wslice(n, cols):
                k = LOAD // cols
                return [w[:, n % 4, :].rearrange("p (k c) -> p k c", k=k) for w in (w_hi, w_lo)]

            def amid(c, k):
                if k == 4:
                    for t in {0: (1,), 1: (2, 3)}.get(c, ()):
                        norm_T(1, t)
                elif 0 <= c - ATT - 2 < 16:
                    prob_v(c - ATT - 2, k - 6)

            def token_block(tag, u, t, src=None, c=None):
                wait_bank(pe, tag)
                for k in range(KT):
                    n = 2 * u + k // 4
                    if c is not None and k in (4, 6, 7):
                        amid(c, k)
                    if u == U_QA and t == 0 and k == 0:
                        pe.wait_ge(first_lo, 1)
                    elif k % 4 == 0 or (u == U_QA and t == 0 and k == 2):
                        pe.wait_ge(lo_ready, n + 1)
                    if k % 4 == 0:
                        if u == U_QA:
                            pe.wait_ge(hT_ready, 2 * t + k // 4 + 1)
                    elif u == U_O0 and t == 0:
                        pe.wait_ge(mrg_ready, k + 1)
                    wh, wl = wslice(n, 512)
                    if src is None:
                        sl = slice(t * P, (t + 1) * P)
                        lh, ll = hT_hi[:, k, sl], hT_lo[:, k, sl]
                    else:
                        lh, ll = src(k, t)
                    ins = mm3(B(tag), lh, ll, wh[:, k % 4, :], wl[:, k % 4, :], k == 0, k == KT - 1)
                ins.then_inc(fullsem(tag), 1)

            def feature_block(tag, u, m, c=None):
                wait_bank(pe, tag)
                for k in range(KT):
                    if c is not None and k in (4, 6, 7):
                        amid(c, k)
                    n = 2 * u + k // 4
                    if k % 4 == 0:
                        pe.wait_ge(lo_ready, n + 1)
                    wh, wl = wslice(n, 512)
                    sl = slice(m * P, (m + 1) * P)
                    ins = mm3(B(tag), wh[:, k % 4, sl], wl[:, k % 4, sl], hT_hi[:, k, :], hT_lo[:, k, :],
                              k == 0, k == KT - 1)
                ins.then_inc(fullsem(tag), 1)

            def norm_T(stage, t):
                pe.wait_ge(xs_ready, 4 * (stage - 1) + t + 1)
                for j in range(2):
                    tag = (f"norm{stage}", t, j)
                    wait_bank(pe, tag)
                    for k in range(4):
                        ins = pe.transpose(B(tag)[:, k * P:(k + 1) * P], xs[:, t % 2, (4 * j + k) * P:(4 * j + k + 1) * P],
                                           ident[:, :])
                    ins.then_inc(fullsem(tag), 1)

            pe.wait_ge(consts, 1)
            for _ in range(8):
                pe.matmul(ps[:, 0, 0:P], ident[:, :], ident[:, :], start=True, stop=True)
            pe.wait_ge(params_loaded, 80)
            pe.transpose(ps[:, 6, 0:96], stg_a[:, :], ident[0:96, 0:96]).then_inc(stage_T, 1)
            norm_T(1, 0)
            pe.wait_ge(conv_loaded, 16)
            pe.transpose(ps[:, 7, 0:88], stg_b[:, :], ident[0:88, 0:88]).then_inc(stage_T, 1)
            for _ in range(12):
                pe.matmul(ps[:, 0, 0:P], ident[:, :], ident[:, :], start=True, stop=True)

            def score(g):
                i, hp = g // 4, g % 4
                n = (i + 1) * P
                if g == 0:
                    pe.wait_ge(consts, 2)
                    wait_freed(pe, ("rope", 6))
                    wait_freed(pe, ("rope", 7))
                for e in range(2):
                    tag = ("score", g, e)
                    wait_bank(pe, tag)
                    rows64 = slice(64 * e, 64 * e + 64)
                    sl = slice(i * P, (i + 1) * P)
                    mm3(B(tag)[:, 0:n], qT_hi[rows64, hp, sl], qT_lo[rows64, hp, sl], kT_hi[rows64, hp, 0:n],
                        kT_lo[rows64, hp, 0:n], True, False)
                    pe.matmul(B(tag)[:, i * P:n], ident_b[:, :], mask_ts[:, :], start=False,
                              stop=True).then_inc(fullsem(tag), 1)

            def prob_T(g):
                i = g // 4
                for e in range(2):
                    tag = ("probT", g, e)
                    wait_bank(pe, tag)
                    wait_freed(pe, ("score", g, e))
                    for j in range(i + 1):
                        ins = pe.transpose(B(tag)[:, j * P:(j + 1) * P], prob[:, e, j * P:(j + 1) * P], ident[:, :])
                    ins.then_inc(fullsem(tag), 1)

            def prob_v(g, e):
                i, h = g // 4, 2 * (g % 4) + e
                tag = ("attn", i)
                if h == 0:
                    wait_bank(pe, tag)
                    wait_freed(pe, ("block", 8 + i))
                wait_freed(pe, ("probT", g, e))
                for j in range(i + 1):
                    ins = pe.matmul(B(tag)[:, h * AD:(h + 1) * AD], probT[:, e, j * P:(j + 1) * P],
                                    va[:, j, h * AD:(h + 1) * AD], start=(j == 0), stop=(j == i))
                ins.then_inc(pv_done, 1)

            def attn_T(i):
                tag = ("attnT", i)
                wait_bank(pe, tag)
                wait_freed(pe, ("attn", i))
                for k in range(4):
                    ins = pe.transpose(B(tag)[:, k * P:(k + 1) * P], tok_a[:, i % 2, k * P:(k + 1) * P], ident[:, :])
                ins.then_inc(fullsem(tag), 1)

            def m_score(g):
                i, hp = g // 2, g % 2
                if hp == 0:
                    tag = ("decay", i)
                    wait_bank(pe, tag)
                    for h in range(MH):
                        ins = pe.matmul(B(tag)[:, h * P:(h + 1) * P], pick[:, h:h + 1].to_broadcast([36, P]),
                                        neg_m[:, i * P:(i + 1) * P], start=True, stop=True)
                    ins.then_inc(fullsem(tag), 1)
                if g == 0:
                    pe.wait_ge(conv_done, 8)
                for e in range(2):
                    tag, h = ("mscore", g, e), 2 * hp + e
                    wait_bank(pe, tag)
                    for j in range(i + 1):
                        ins = pe.matmul(B(tag)[:, j * P:(j + 1) * P], kmT[:, h, j * P:(j + 1) * P],
                                        qmT[:, h, i * P:(i + 1) * P], start=True, stop=True)
                    ins.then_inc(fullsem(tag), 1)

            def m_num(g):
                i, hp, tag = g // 2, g % 2, ("mnum", g)
                wait_bank(pe, tag)
                if g == 0:
                    pe.wait_ge(ones_col, 1)
                    wait_freed(pe, ("block", 22))
                    wait_freed(pe, ("block", 23))
                for e in range(2):
                    h = 2 * hp + e
                    wait_freed(pe, ("mscore", g, e))
                    for j in range(i + 1):
                        ins = pe.matmul(B(tag)[:, e * (MD + 1):(e + 1) * (MD + 1)], prob[:, e, j * P:(j + 1) * P],
                                        vm[:, j, h, :], start=(j == 0), stop=(j == i))
                ins.then_inc(fullsem(tag), 1)

            def m_T(i):
                tag = ("mT", i)
                wait_bank(pe, tag)
                pe.wait_ge(hm_ready, i + 1)
                for k in range(4):
                    ins = pe.transpose(B(tag)[:, k * P:(k + 1) * P], h_tok(i)[:, k * P:(k + 1) * P], ident[:, :])
                ins.then_inc(fullsem(tag), 1)

            for c in range(NBLK):
                u, m = c // 4, c % 4
                tag = ("block", c)
                if u in (U_QM, U_KM, U_GA0, U_GM0, U_GA1):
                    feature_block(tag, u, m, c=c)
                else:
                    token_block(tag, u, m, c=c)
                if 2 <= c <= 9:
                    rt = ("rope", c - 2)
                    wait_bank(pe, rt)
                    if c == 2:
                        pe.wait_ge(params_ready, 2)
                    pe.wait_ge(rope_done, c - 1)
                    for k in range(4):
                        ins = pe.transpose(B(rt)[:, k * P:(k + 1) * P], qr[:, c % 2, k * P:(k + 1) * P], ident[:, :])
                    ins.then_inc(fullsem(rt), 1)
                if c == 5:
                    gi = ("gates_if",)
                    wait_bank(pe, gi)
                    pe.wait_ge(wif_ready, 1)
                    for k in range(KT):
                        ins = mm3(B(gi), wif_hi[:, k, :], wif_lo[:, k, :], hT_hi[:, k, :], hT_lo[:, k, :],
                                  k == 0, k == KT - 1)
                    ins.then_inc(fullsem(gi), 1)
                if c == 11:
                    ci = ("cols_if",)
                    wait_bank(pe, ci)
                    pe.wait_ge(rows_ready, 1)
                    at = 0
                    for i in range(NT):
                        for j in range(i + 1):
                            pe.transpose(B(ci)[:, at:at + 4], rows[:, 4 + i, j * P:(j + 1) * P], ident[0:4, 0:4])
                            at += 4
                    for i in range(NT):
                        ins = pe.transpose(B(ci)[:, at:at + 4], rows[:, 0, i * P:(i + 1) * P], ident[0:4, 0:4])
                        at += 4
                    ins.then_inc(fullsem(ci), 1)
                if 0 <= c - ATT < 16:
                    score(c - ATT)
                if 0 <= c - ATT - 1 < 16:
                    prob_T(c - ATT - 1)
                if 0 <= c - ATT - 6 <= 12 and (c - ATT - 6) % 4 == 0:
                    attn_T((c - ATT - 6) // 4)
                if 0 <= c - MLS < 8:
                    m_score(c - MLS)
                if 0 <= c - MLS - 4 <= 6 and (c - MLS - 4) % 2 == 0:
                    m_T((c - MLS - 4) // 2)
                if 0 <= c - MLS - 1 < 8:
                    m_num(c - MLS - 1)

            def branches(u, n):
                m = n % 4
                for s, (src_hi, src_lo) in enumerate(((atT_hi, atT_lo), (hmT_hi, hmT_lo))):
                    tag = ("y", n, s)
                    wait_bank(pe, tag)
                    if n == 0:
                        if s == 0:
                            wait_freed(pe, ("attnT", 3))
                        else:
                            pe.wait_ge(hmT_ready, 4)
                    pe.wait_ge(lo_ready, 2 * u + s + 1)
                    wh, wl = wslice(2 * u + s, 512)
                    sl = slice(m * P, (m + 1) * P)
                    for k in range(4):
                        ins = mm3(B(tag), wh[:, k, sl], wl[:, k, sl], src_hi[:, k, :], src_lo[:, k, :], k == 0, k == 3)
                    ins.then_inc(fullsem(tag), 1)

            for n in range(4):
                branches(U_B0, n)
            for m in range(4):
                feature_block(("gate", m), U_GM1, m)
            for n in range(4, 8):
                branches(U_B1, n)

            def merged(k, t):
                hi, lo = ((mrg_hi0, mrg_lo0), (mrg_hi1, mrg_lo1))[k // 4]
                sl = slice(t * P, (t + 1) * P)
                return hi[:, k % 4, sl], lo[:, k % 4, sl]

            pe.wait_ge(mrg_ready, 5)
            for t in range(NT):
                for n in range(2):
                    token_block(("out", t, n), U_O0 + n, t, merged)
                    if n == 0 and t >= 1:
                        norm_T(2, t - 1)
            def up(f, n, it):
                pe.wait_ge(lo_ready, 4 * it + (n + 1))
                for s in range(2):
                    bank, k0, _ = plan[("up", f, s)]
                    pe.wait_ge(bank_free[bank], 2 * it + k0)
                    wh, wl = [w[:, n % 4, s * 1024:(s + 1) * 1024].rearrange("p (k c) -> p k c", k=KT) for w in (w_hi, w_lo)]
                    for k in range(KT):
                        ins = mm3(ps[:, bank, :], wh[:, k, :], wl[:, k, :], hT_hi[:, k, :], hT_lo[:, k, :],
                                  k == 0, k == KT - 1)
                    ins.then_inc(bank_full[bank], 1)

            def up_first():
                n = N_UP[0]
                pe.wait_ge(lo_ready, n + 1)
                for part in range(2):
                    cols = (slice(0, 3 * P), slice(3 * P, SEQ))[part]
                    if part == 0:
                        pe.wait_ge(hT_ready, 14)
                    else:
                        pe.wait_ge(hT_ready, 16)
                    for s in range(2):
                        tag = ("up", 0, s)
                        if part == 0:
                            wait_bank(pe, tag)
                        wh, wl = [w[:, n % 4, s * 1024:(s + 1) * 1024].rearrange("p (k c) -> p k c", k=KT) for w in (w_hi, w_lo)]
                        for k in range(KT):
                            ins = mm3(B(tag)[:, cols], wh[:, k, :], wl[:, k, :], hT_hi[:, k, cols], hT_lo[:, k, cols],
                                      k == 0, k == KT - 1)
                            if part == 0 and s == 0 and k == KT - 1:
                                norm_T(2, NT - 1)
                        if part == 1:
                            ins.then_inc(fullsem(tag), 1)

            up_first()
            for g in range(2):
                f0, n0 = g * GROUP[0], N_UP[g]
                first = 0
                if g == 0:
                    for j in range(1, 4):
                        up(f0 + j, n0 + j, 0)
                    first = 4
                loops = (GROUP[g] - first) // 4
                with pe.Fori(0, loops) as it:
                    for j in range(4):
                        up(f0 + first + j, n0 + first + j, it)
                for j in range(first + 4 * loops, GROUP[g]):
                    up(f0 + j, n0 + j, 0)
                nd = GROUP[g] // 2

                def down(d, t, c):
                    tag, n = ("down", g, t, c), N_DOWN[g] + d
                    if d == 0:
                        wait_bank(pe, tag)
                    wh, wl = wslice(n, 1024)
                    sl, cs = slice(t * P, (t + 1) * P), slice(c * 512, (c + 1) * 512)
                    for k in range(2):
                        ins = mm3(B(tag), act_hi[:, 2 * d + k, sl], act_lo[:, 2 * d + k, sl], wh[:, k, cs], wl[:, k, cs],
                                  d == 0 and k == 0, d == nd - 1 and k == 1)
                    if d == nd - 1:
                        ins.then_inc(fullsem(tag), 1)
                    return ins

                together = nd - 1 if g == 0 else nd - 2
                for d in range(together):
                    pe.wait_ge(lo_ready, N_DOWN[g] + d + 1)
                    pe.wait_ge(act_ready, f0 + 2 * d + 2)
                    for t in (2, 3, 0, 1) if d == 0 else range(NT):
                        for c in range(2):
                            ins = down(d, t, c)
                    ins.then_inc(down_used, 1)
                pe.wait_ge(lo_ready, N_DOWN[g] + nd)
                pe.wait_ge(act_ready, f0 + 2 * nd)
                for t in range(NT):
                    for c in range(2):
                        for d in range(together, nd):
                            down(d, t, c)


_INS = ["x", "positions", "norm_mix_g", "w_in", "conv_mlstm", "i_bias", "f_bias", "mlstm_norm_g", "w_branch_attn",
        "w_branch_mlstm", "w_out", "norm_ffn_g", "w_up", "conv_ffn", "w_down", "norm_final_g"]


def kernel(**inputs):
    import numpy as _np
    import concourse.bacc as _bacc
    from concourse import mybir as _mybir
    from concourse.bass_utils import run_bass_kernel_spmd as _run

    nc = _bacc.Bacc("TRN2", target_bir_lowering=False, num_devices=1)
    arrays, args = {}, []
    for name in _INS:
        a = _np.ascontiguousarray(inputs[name])
        arrays[f"in_{name}"] = a
        args.append(nc.dram_tensor(f"in_{name}", a.shape, _mybir.dt.from_np(a.dtype), kind="ExternalInput").ap())
    freq = (10000.0 ** (-_np.arange(32) / 32.0)).astype(_np.float32)[None]
    arrays["inv_freq"] = freq
    args.append(nc.dram_tensor("inv_freq", freq.shape, _mybir.dt.float32, kind="ExternalInput").ap())
    args.append(nc.dram_tensor("out_0", (1, SEQ, D), _mybir.dt.float32, kind="ExternalOutput").ap())
    build(nc, *args)
    r = _run(nc, [arrays], core_ids=[0])
    return r.results[0]["out_0"]
```
